# Optimizing a Trainium2 kernel written in Bass

```python
import math
import jax, jax.numpy as jnp
from jax import lax
import numpy as np

D_MODEL = 2048
BATCH = 1
SEQ = 256
DEPTH = 1
DEC_BATCH = 8
DEC_SEQ = 8
PAST_LEN = 256
PAGE_SIZE = 128

MIX_WIDTH = D_MODEL
ATTN_WIDTH = MIX_WIDTH // 2
POOL_WIDTH = MIX_WIDTH - ATTN_WIDTH
N_HEADS = 8
HEAD_DIM = ATTN_WIDTH // (2 * N_HEADS)
V_DIM = 2 * HEAD_DIM
ROT_DIM = HEAD_DIM // 4
ROPE_THETA = 500000.0
POOL_WINDOWS = (2, 4, 8, 16)
N_POOL_GROUPS = len(POOL_WINDOWS)
POOL_GROUP_WIDTH = POOL_WIDTH // N_POOL_GROUPS
POOL_HIST = max(POOL_WINDOWS) - 1
IN_WIDTH = 3 * ATTN_WIDTH + POOL_WIDTH
D_FF = 4 * D_MODEL
N_MOD = 6
Q_BLOCK = 128
EPS = 1e-6

kernel_name = "hymba_diffattn_pool_decoder_step"

def rms_norm(x, g):
    xf = x.astype(jnp.float32)
    y = xf * lax.rsqrt(jnp.mean(xf * xf, axis=-1, keepdims=True) + EPS)
    return (y * g.astype(jnp.float32)).astype(x.dtype)

def rotary(x, pos):
    inv = 1.0 / (ROPE_THETA ** (jnp.arange(0, ROT_DIM, 2, dtype=jnp.float32) / ROT_DIM))
    ang = pos.astype(jnp.float32)[:, None] * inv[None, :]
    cos = jnp.cos(ang)[:, None, None, :].astype(x.dtype)
    sin = jnp.sin(ang)[:, None, None, :].astype(x.dtype)
    half = ROT_DIM // 2
    x1 = x[..., :half]
    x2 = x[..., half:ROT_DIM]
    return jnp.concatenate([x1 * cos - x2 * sin, x2 * cos + x1 * sin, x[..., ROT_DIM:]], axis=-1)

def ada_modulation(c, w_ada, b_ada):
    m = jax.nn.silu(c) @ w_ada + b_ada
    return jnp.split(m[:, None, :], N_MOD, axis=-1)

def mixer_inputs(x, shift, scale, g_pre, w_in, pos):
    b, t = x.shape[:2]
    h = rms_norm(x, g_pre) * (1.0 + scale) + shift
    z = h @ w_in
    q, k, v, u = jnp.split(z, [ATTN_WIDTH, 2 * ATTN_WIDTH, 3 * ATTN_WIDTH], axis=-1)
    q = rotary(q.reshape(b, t, N_HEADS, 2, HEAD_DIM), pos)
    k = rotary(k.reshape(b, t, N_HEADS, 2, HEAD_DIM), pos)
    v = v.reshape(b, t, N_HEADS, V_DIM)
    return q, k, v, u

def diff_attend(q, k, v, q_pos, k_pos, lam):
    s = jnp.einsum('bqhmd,bkhmd->bhmqk', q, k).astype(jnp.float32) * (HEAD_DIM ** -0.5)
    mask = k_pos[None, :] <= q_pos[:, None]
    p = jax.nn.softmax(jnp.where(mask, s, -jnp.inf), axis=-1)
    a = p[:, :, 0] - lam * p[:, :, 1]
    return jnp.einsum('bhqk,bkhe->bqhe', a.astype(v.dtype), v)

def prompt_attention(q, k, v, pos, lam):
    b, t = q.shape[:2]
    nb = t // Q_BLOCK
    qb = q.reshape(b, nb, Q_BLOCK, N_HEADS, 2, HEAD_DIM).swapaxes(0, 1)
    pb = pos.reshape(nb, Q_BLOCK)
    out = lax.map(lambda a: diff_attend(a[0], k, v, a[1], pos, lam), (qb, pb))
    return out.swapaxes(0, 1).reshape(b, t, N_HEADS, V_DIM)

def pool_mix(u_ext, pos_ext, n_out, w_pool, pool_scale):
    b, L = u_ext.shape[:2]
    uf = u_ext.astype(jnp.float32).reshape(b, L, N_POOL_GROUPS, POOL_GROUP_WIDTH)
    cs = jnp.cumsum(uf, axis=1)
    outs = []
    for g, w in enumerate(POOL_WINDOWS):
        c = cs[:, :, g]
        c_prev = jnp.pad(c, ((0, 0), (w, 0), (0, 0)))[:, :L]
        cnt = jnp.minimum(w, pos_ext + 1).astype(jnp.float32)[None, :, None]
        outs.append((c - c_prev) / cnt - uf[:, :, g])
    pooled = jnp.stack(outs, axis=2)[:, L - n_out:]
    y = jnp.einsum('btgc,gcd->btgd', pooled.astype(u_ext.dtype), w_pool)
    return y.reshape(b, n_out, POOL_WIDTH) * pool_scale

def mixer_output(x, attn, pooled, gate, g_subln, lam_init, w_out, g_post):
    b, t = x.shape[:2]
    a = rms_norm(attn, g_subln) * (1.0 - lam_init)
    m = jnp.concatenate([a.reshape(b, t, ATTN_WIDTH), pooled], axis=-1) @ w_out
    return x + gate * rms_norm(m, g_post)

def ffn_block(x, shift, scale, gate, g_pre, w1, w2, g_post):
    h = rms_norm(x, g_pre) * (1.0 + scale) + shift
    f = jnp.square(jax.nn.relu(h @ w1)) @ w2
    return x + gate * rms_norm(f, g_post)

def setup_inputs(seed: int = 0) -> dict:
    key = jax.random.key(seed)
    ks = jax.random.split(key, 28)
    n_pages = PAST_LEN // PAGE_SIZE
    n_used = DEC_BATCH * n_pages
    n_phys = (n_used * 5) // 4

    def nrm(k, shape, s):
        return jax.random.normal(k, shape, jnp.float32) * s

    def gain(k, shape):
        return 1.0 + 0.05 * jax.random.normal(k, shape, jnp.float32)

    page_table = jax.random.permutation(ks[7], n_phys)[:n_used].reshape(DEC_BATCH, n_pages).astype(jnp.int32)
    return {
        "x_prompt": nrm(ks[0], (BATCH, SEQ, D_MODEL), 1.0),
        "x_sample": nrm(ks[1], (DEC_BATCH, DEC_SEQ, D_MODEL), 1.0),
        "cache_k": nrm(ks[2], (DEPTH, n_phys, PAGE_SIZE, N_HEADS, 2 * HEAD_DIM), 1.0),
        "cache_v": nrm(ks[3], (DEPTH, n_phys, PAGE_SIZE, N_HEADS, V_DIM), 1.0),
        "state_pool": nrm(ks[4], (DEPTH, DEC_BATCH, POOL_HIST, POOL_WIDTH), 1.0),
        "page_table": page_table,
        "c_prompt": nrm(ks[5], (BATCH, D_MODEL), 1.0),
        "c_sample": nrm(ks[6], (DEC_BATCH, D_MODEL), 1.0),
        "w_ada": nrm(ks[8], (DEPTH, D_MODEL, N_MOD * D_MODEL), 0.5 * D_MODEL ** -0.5),
        "b_ada": nrm(ks[9], (DEPTH, N_MOD * D_MODEL), 0.01),
        "g_pre_mix": gain(ks[10], (DEPTH, D_MODEL)),
        "w_in": nrm(ks[11], (DEPTH, D_MODEL, IN_WIDTH), D_MODEL ** -0.5),
        "lambda_q1": nrm(ks[12], (DEPTH, HEAD_DIM), 0.1),
        "lambda_k1": nrm(ks[13], (DEPTH, HEAD_DIM), 0.1),
        "lambda_q2": nrm(ks[14], (DEPTH, HEAD_DIM), 0.1),
        "lambda_k2": nrm(ks[15], (DEPTH, HEAD_DIM), 0.1),
        "g_subln": gain(ks[16], (DEPTH, V_DIM)),
        "w_pool": nrm(ks[17], (DEPTH, N_POOL_GROUPS, POOL_GROUP_WIDTH, POOL_GROUP_WIDTH), POOL_GROUP_WIDTH ** -0.5),
        "pool_scale": gain(ks[18], (DEPTH, POOL_WIDTH)),
        "w_out": nrm(ks[19], (DEPTH, MIX_WIDTH, D_MODEL), MIX_WIDTH ** -0.5),
        "g_post_mix": gain(ks[20], (DEPTH, D_MODEL)),
        "g_pre_ffn": gain(ks[21], (DEPTH, D_MODEL)),
        "w_ff1": nrm(ks[22], (DEPTH, D_MODEL, D_FF), D_MODEL ** -0.5),
        "w_ff2": nrm(ks[23], (DEPTH, D_FF, D_MODEL), D_FF ** -0.5),
        "g_post_ffn": gain(ks[24], (DEPTH, D_MODEL)),
    }

def reference(x_prompt, x_sample, cache_k, cache_v, state_pool, page_table, c_prompt, c_sample,
              w_ada, b_ada, g_pre_mix, w_in, lambda_q1, lambda_k1, lambda_q2, lambda_k2, g_subln,
              w_pool, pool_scale, w_out, g_post_mix, g_pre_ffn, w_ff1, w_ff2, g_post_ffn):
    pos_p = jnp.arange(SEQ, dtype=jnp.int32)
    pos_s = PAST_LEN + jnp.arange(DEC_SEQ, dtype=jnp.int32)
    pos_past = jnp.arange(PAST_LEN, dtype=jnp.int32)
    pos_keys_s = jnp.concatenate([pos_past, pos_s])
    pos_pool_s = PAST_LEN - POOL_HIST + jnp.arange(POOL_HIST + DEC_SEQ, dtype=jnp.int32)

    xp, xs = x_prompt, x_sample
    kp_l, vp_l, sp_l, ks_l, vs_l, ss_l = [], [], [], [], [], []
    for l in range(DEPTH):
        lam_init = 0.8 - 0.6 * math.exp(-0.3 * l)
        lam = (jnp.exp(jnp.sum(lambda_q1[l] * lambda_k1[l]).astype(jnp.float32))
               - jnp.exp(jnp.sum(lambda_q2[l] * lambda_k2[l]).astype(jnp.float32)) + lam_init)
        mp = ada_modulation(c_prompt, w_ada[l], b_ada[l])
        ms = ada_modulation(c_sample, w_ada[l], b_ada[l])

        q, k, v, u = mixer_inputs(xp, mp[0], mp[1], g_pre_mix[l], w_in[l], pos_p)
        attn = prompt_attention(q, k, v, pos_p, lam)
        pooled = pool_mix(u, pos_p, SEQ, w_pool[l], pool_scale[l])
        xp = mixer_output(xp, attn, pooled, mp[2], g_subln[l], lam_init, w_out[l], g_post_mix[l])
        xp = ffn_block(xp, mp[3], mp[4], mp[5], g_pre_ffn[l], w_ff1[l], w_ff2[l], g_post_ffn[l])
        kp_l.append(k.reshape(BATCH, SEQ, N_HEADS, 2 * HEAD_DIM))
        vp_l.append(v)
        sp_l.append(u[:, SEQ - POOL_HIST:])

        q, k, v, u = mixer_inputs(xs, ms[0], ms[1], g_pre_mix[l], w_in[l], pos_s)
        k_past = cache_k[l, page_table].reshape(DEC_BATCH, PAST_LEN, N_HEADS, 2, HEAD_DIM)
        v_past = cache_v[l, page_table].reshape(DEC_BATCH, PAST_LEN, N_HEADS, V_DIM)
        k_all = jnp.concatenate([k_past.astype(k.dtype), k], axis=1)
        v_all = jnp.concatenate([v_past.astype(v.dtype), v], axis=1)
        attn = diff_attend(q, k_all, v_all, pos_s, pos_keys_s, lam)
        u_ext = jnp.concatenate([state_pool[l].astype(u.dtype), u], axis=1)
        pooled = pool_mix(u_ext, pos_pool_s, DEC_SEQ, w_pool[l], pool_scale[l])
        xs = mixer_output(xs, attn, pooled, ms[2], g_subln[l], lam_init, w_out[l], g_post_mix[l])
        xs = ffn_block(xs, ms[3], ms[4], ms[5], g_pre_ffn[l], w_ff1[l], w_ff2[l], g_post_ffn[l])
        ks_l.append(k.reshape(DEC_BATCH, DEC_SEQ, N_HEADS, 2 * HEAD_DIM))
        vs_l.append(v)
        ss_l.append(u_ext[:, DEC_SEQ:])

    k_prompt = jnp.stack(kp_l)
    v_prompt = jnp.stack(vp_l)
    pool_prompt = jnp.stack(sp_l)
    k_sample = jnp.stack(ks_l)
    v_sample = jnp.stack(vs_l)
    pool_sample = jnp.stack(ss_l)
    return (xp, xs, k_prompt, v_prompt, pool_prompt, k_sample, v_sample, pool_sample)


_drawn_inputs = setup_inputs


def setup_inputs(seed=0):
    import zlib

    import numpy as np

    out = dict(_drawn_inputs(seed))
    spreads = {}
    factors = {'b_ada': 3.722,
     'lambda_q1': 4.184,
     'lambda_q2': 189.112,
     'lambda_k2': 3.123,
     'g_subln': 5.7,
     'pool_scale': 5.326,
     'g_post_mix': 3.906,
     'g_pre_ffn': 3.647,
     'g_post_ffn': 4.078}
    for name, (base, spread) in spreads.items():
        noise = np.random.default_rng([zlib.crc32(name.encode()), seed]).standard_normal(out[name].shape)
        drawn = base * np.exp(spread * noise) if base else spread * noise
        out[name] = __import__('jax').numpy.asarray(drawn.astype(out[name].dtype))
    for name, factor in factors.items():
        out[name] = (out[name] * factor).astype(out[name].dtype)
    return out
```

```python
import concourse.bass as bass
from concourse import mybir
import numpy as np

P = 128
D = 2048
KT = D // P
NP_, NS = 256, 64
T = NP_ + NS
SEQS, STEPS = 8, 8
NSEQ = 1 + SEQS
HEADS, HD = 8, 64
PAST, PAGE, PAGES = 256, 128, 2
HIST = 15
UP = HIST + NP_
US = (HIST + STEPS) * SEQS
POOL_GROUPS = 4
LAM_INIT = 0.8 - 0.6
SCALE = HD ** -0.5
EPS = 1e-6
MASKED = -1e30
GROUPS = 4

ADA_FIRST = 8
SB_V, SB_QK, SB_U, SB_OUT = 2, 4, 2, 4
STREAM = 4 * ADA_FIRST + 8 * (SB_V + SB_QK + SB_U + SB_OUT) + 36 * GROUPS
SUPER = [1, 3, 5, 7]
PLAIN = [0, 1, 2, 3]

C_ID, C_DIAG = 0, 128
C_NEWMASK, C_PICK9 = 256, 512
C_PICK64, C_M0, C_M1 = 521, 585, 586
C_FIX, C_END = 587, 651

G_PRE_MIX, G_POST_MIX, G_PRE_FFN, G_POST_FFN, G_POOL, G_SUB, G_END = 0, 16, 32, 48, 64, 72, 73


class Steps:

    def __init__(self, eng, sem):
        self.eng, self.sem, self.base, self.n = eng, sem, 0, 0

    def mark(self, instruction):
        instruction.then_inc(self.sem, 1)
        self.n += 1

    def wait(self):
        self.eng.wait_ge(self.sem, self.base + self.n)

    def then(self, instruction):
        self.mark(instruction)
        self.wait()

    def enter(self, i, per):
        self.start, self.per = self.base + self.n, per
        self.base, self.n = self.start + i * per, 0

    def leave(self, turns):
        assert self.n == self.per, self.n
        self.base, self.n = self.start + turns * self.per, 0


def decoder_step(nc, stream, x_cm, c_cm, kc, vc, table_pg, state_cm, w_pool, bias, gains, lam4, trig, consts,
                 y_out, k_out, v_out, poolp_out, pools_out):
    f32, f32r, i32 = mybir.dt.float32, mybir.dt.float32r, mybir.dt.int32
    ALU, ACT, AX = mybir.AluOpType, mybir.ActivationFunctionType, mybir.AxisListType
    ds = bass.ds

    base = (nc.sbuf_base + 31) // 32 * 32
    cursor = [base]

    def at(name, shape, dtype, offset):
        return nc.alloc_sbuf_tensor_at(name, shape, dtype, offset=offset)

    def region(nbytes):
        start = cursor[0]
        cursor[0] += (nbytes + 31) // 32 * 32
        assert cursor[0] <= nc.sbuf_usable_end, cursor[0]
        return start

    def own(name, shape, dtype=f32):
        return at(name, shape, dtype, region(4 * int(np.prod(shape[1:]))))

    raw = [own(f"raw{s}", [P, 2048]) for s in range(4)]
    w_hi = [own(f"w_hi{q}", [P, 1024], f32r) for q in range(4)]
    w_lo = [own(f"w_lo{q}", [P, 1024], f32r) for q in range(4)]
    R_H = region(2 * KT * T * 4)
    h_hi, h_lo = at("h_hi", [P, KT, T], f32r, R_H), at("h_lo", [P, KT, T], f32r, R_H + KT * T * 4)
    pool_w = at("pool_w", [P, POOL_GROUPS, 2, 256], f32, R_H)
    pool_y = at("pool_y", [P, 2, T], f32, R_H + 8192)
    last_squares = at("last_squares", [P, KT, T], f32, R_H)
    R_C = region(2 * KT * T * 4)
    m_hi, m_lo = at("m_hi", [P, KT, T], f32r, R_C), at("m_lo", [P, KT, T], f32r, R_C + KT * T * 4)
    v_cm = at("v_cm", [P, HEADS, T], f32, R_C)
    k_pages = at("k_pages", [P, 2, PAGES, HEADS * PAGE], f32, R_C)
    v_pages = at("v_pages", [P, 2, PAGES, HEADS * P], f32, R_C + 16384)
    v_rows = at("v_rows", [P, 2, HEADS * P], f32, R_C + 32768)
    squares = at("squares", [P, KT, T], f32, R_C)
    normed = at("normed", [P, KT, T], f32, R_C + KT * T * 4)
    R_X = region(KT * T * 4)
    x = at("x", [P, KT, T], f32, R_X)
    u_p = at("u_p", [P, HEADS, UP], f32, R_X)
    u_s = at("u_s", [P, HEADS, US], f32, R_X + HEADS * UP * 4)
    R_XS = R_X + HEADS * (UP + US) * 4
    probs = at("probs", [P, 2, 384], f32, R_XS)
    probs_t = at("probs_t", [P, 384], f32, R_XS + 3072)
    dprobs = at("dprobs", [P, 2, PAST + NS], f32, R_XS)
    dprobs_t = at("dprobs_t", [P, 2, PAGES, 64], f32, R_XS + 3072)
    R_A = region(KT * T * 4)
    back = at("back", [P, KT, T], f32, R_A)
    q_cm, k_cm = back[:, 0:HEADS, :], back[:, HEADS:KT, :]
    sub_sq = k_cm.rearrange("p h t -> p (h t)")
    v_new = own("v_new", [NS, HEADS * P])
    ada_rows = own("ada_rows", [P, 512])
    R_S = region(5120)
    rope = [at(f"rope{n}", [P, T], f32, R_S + n * T * 4) for n in range(4)]
    q_pick = at("q_pick", [P, 2, HEADS, 32], f32, R_S)
    dnew_t = at("dnew_t", [NS, HEADS, NS], f32, R_S + 2048)
    out_sq = [at(f"out_sq{n}", [P, T], f32, R_S + n * T * 4) for n in range(2)]
    sq_sum = at("sq_sum", [P, T], f32, R_S + 2 * T * 4)
    relu = [at(f"relu{n}", [P, T], f32, R_S + n * T * 4) for n in range(2)]
    relu2 = [at(f"relu2{n}", [P, T], f32, R_S + (2 + n) * T * 4) for n in range(2)]
    R_T = region(3 * T * 4)
    cos_sin = at("cos_sin", [P, 2, T], f32, R_T)
    rstd = at("rstd", [P, T], f32, R_T + 2 * T * 4)
    win = [at(f"win{n}", [P, UP + US], f32, R_T + n * 1824) for n in range(2)]
    mod = own("mod", [P, 24, 4, NSEQ])
    gate = own("gate", [P, KT, NSEQ])
    tab = own("tab", [P, C_END])
    gain = own("gain", [P, G_END])
    ada_bias = own("ada_bias", [P, 24, 4])
    ones = own("ones", [P, P])
    silu_c = own("silu_c", [P, KT, NSEQ])
    lam_in = own("lam_in", [HD, 4])
    lam_pr = own("lam_pr", [HD, 2])
    small = own("small", [P, 48])
    pages_sb = own("pages_sb", [1, SEQS * PAGES], i32)

    eps = small[:, 0:1]
    lam_e = small[:, 1:3]
    coef4 = small[:, 3:7]
    coefd = small[:, 7:8]
    nmax, nb4, sums, rsum = small[:, 8:12], small[:, 12:16], small[:, 16:20], small[:, 20:24]
    c_exp = at("c_exp", [P, KT, NSEQ], f32, R_S)
    ident = tab[:, C_ID:C_ID + P]
    scr = {"dn": small[:, 24:26]}

    bank = [nc.alloc_psum_tensor(f"bank{n}", [P, 512], f32) for n in range(8)]
    ADA, MODT = bank[2], bank[4]

    def S(name):
        return nc.alloc_semaphore(name)

    raw_loaded = [S(f"raw_loaded{s}") for s in range(4)]
    slot_used = [S(f"slot_used{s}") for s in range(4)]
    half_free = S("half_free")
    bank_free = [S("bank_free0"), S("bank_free1")]
    hi_ready = S("hi_ready")
    x_loaded, c_loaded, tables_loaded, pg_loaded = S("x_loaded"), S("c_loaded"), S("tables_loaded"), S("pg_loaded")
    ones_set, c_exped, silu_done, lam_pred, lam_summed, lam_exped = [S(n) for n in (
        "ones_set", "c_exped", "silu_done", "lam_pred", "lam_summed", "lam_exped")]
    squared, meaned, rooted, normed_s, rstd_s = S("squared"), S("meaned"), S("rooted"), S("normed_s"), S("rstd_s")
    ada_copied, sel_done, mod_done = S("ada_copied"), S("sel_done"), S("mod_done")
    gate_done = S("gate_done")
    prompt_mod, sample_mod, h_hi_s, h_ready = S("prompt_mod"), S("sample_mod"), S("h_hi_s"), S("h_ready")
    roped = S("roped")
    dstep, astep, pstep = S("dstep"), S("astep"), S("pstep")
    vt_turned, vt_evac, v_stored, k_stored = S("vt_turned"), S("vt_evac"), S("v_stored"), S("k_stored")
    k_loaded, v_loaded = [S("k_loaded0"), S("k_loaded1")], [S("v_loaded0"), S("v_loaded1")]
    s_done, negmax, exped, a_ready, t_done, at_ready, pv_done, o_done = [S(n) for n in (
        "s_done", "negmax", "exped", "a_ready", "t_done", "at_ready", "pv_done", "o_done")]
    q_ready, ds_done, dnegmax, dexped, da_ready, dt_done, dat_ready, dpv_done, dall_done = [S(n) for n in (
        "q_ready", "ds_done", "dnegmax", "dexped", "da_ready", "dt_done", "dat_ready", "dpv_done", "dall_done")]
    attn_raw, sub_squared, sub_mean, sub_root, sub_scaled, sub_hi, attn_ready = [S(n) for n in (
        "attn_raw", "sub_squared", "sub_mean", "sub_root", "sub_scaled", "sub_hi", "attn_ready")]
    hist_set, state_loaded, pool_stored, pooled, poolw_loaded, y_done, y_scaled, pooled_ready = [S(n) for n in (
        "hist_set", "state_loaded", "pool_stored", "pooled", "poolw_loaded", "y_done", "y_scaled", "pooled_ready")]
    sq_ready, sq_summed = S("sq_ready"), S("sq_summed")
    hidden = S("hidden")
    x_again, back_scaled, prompt_res, sample_res = S("x_again"), S("back_scaled"), S("prompt_res"), S("sample_res")
    y_stored = S("y_stored")

    def use_of(use, off):
        return off % 4, use + off // 4

    def wait_raw(eng, use, off):
        slot, u = use_of(use, off)
        eng.wait_ge(raw_loaded[slot], 16 * (u + 1))

    def wait_chunk(eng, c4, j):
        eng.wait_ge(half_free, 8 * c4 + (2 * j + 6))

    def super_use(sb):
        return ADA_FIRST + 2 * sb

    def ffn_use(g):
        return ADA_FIRST + 2 * (SB_V + SB_QK + SB_U + SB_OUT) + 9 * g

    FFN_C4 = SB_V + SB_QK + SB_U + SB_OUT
    N_SB = FFN_C4

    def seq_view(ap):
        return ap.rearrange("p k (q b) -> p k q b", b=SEQS)

    def bcast_seq(ap9):
        k = ap9.shape[1]
        return ap9[:, :, 1:NSEQ].unsqueeze(2).to_broadcast([P, k, STEPS, SEQS])

    def mod_of(first_block):
        return mod[:, first_block:first_block + 4, :, :].rearrange("p b t s -> p (b t) s")

    GATE1, SCALE2, SHIFT2, GATE2 = 8, 12, 16, 20

    block = nc.Block()
    block.__enter__()

    @block.sync
    def _(sp):
        with sp.Fori(0, STREAM // 4) as i:
            for s in range(4):
                sp.wait_ge(slot_used[s], 2 * i + 2)
                sp.dma_start(raw[s][:, :], stream[ds(4 * i + s, 1), :, :].rearrange("a p n -> p (a n)")).then_inc(
                    raw_loaded[s], 16)
        for g in range(4):
            sp.wait_ge(prompt_res, 8 + g + 1 - 4)
            sp.wait_ge(sample_res, 8 + g + 1 - 4)
            sp.dma_start(y_out[:, 4 * g:4 * g + 4, :], x[:, 4 * g:4 * g + 4, :]).then_inc(y_stored, 16)
        sp.wait_ge(y_stored, 64)

    @block.scalar
    def _(act):
        mine = Steps(act, astep)
        act.dma_start(silu_c[:, :, :], c_cm).then_inc(c_loaded, 16)
        for dst, src in ((tab[:, :], consts), (gain[:, :], gains), (ada_bias[:, :, :], bias), (lam_in[:, :], lam4),
                         (cos_sin[:, :, :], trig)):
            act.dma_start(dst, src).then_inc(tables_loaded, 16)
        act.dma_start(x[:, :, :], x_cm).then_inc(x_loaded, 16)

        act.wait_ge(c_loaded, 16)
        act.activation(c_exp[:, :, :], silu_c[:, :, :], ACT.Exp, scale=-1.0).then_inc(c_exped, 1)
        act.wait_ge(lam_summed, 1)
        act.activation(lam_e, bank[6][:, 0:2], ACT.Exp, scale=float(P)).then_inc(lam_exped, 1)

        def square_all(src, loaded, need):
            for g in range(4):
                act.wait_ge(loaded, need(g))
                act.activation(squares[:, 4 * g:4 * g + 4, :], src[:, 4 * g:4 * g + 4, :], ACT.Square).then_inc(squared, 1)

        def root(src, need_mean, width):
            act.wait_ge(meaned, need_mean)
            act.activation(rstd[:, :], src, ACT.Sqrt, bias=eps, scale=1.0 / width).then_inc(rooted, 1)

        def ada_copy(nb, use, off):
            slot, u = use_of(use, off)
            act.wait_ge(slot_used[slot], 2 * u + 4)
            act.wait_ge(sel_done, nb + 1)
            act.activation(ada_rows[:, :], ADA[:, :], ACT.Copy).then_inc(ada_copied, 1)

        def hi_half(c4, use, off, j, h):
            slot, u = use_of(use, off)
            act.wait_ge(raw_loaded[slot], 16 * (u + 1))
            act.wait_ge(half_free, 8 * c4 + (2 * j + h + 1))
            act.activation(w_hi[2 * (j % 2) + h][:, :], raw[slot][:, h * 1024:(h + 1) * 1024], ACT.Copy).then_inc(
                hi_ready, 1)

        def block4(c4, use, offs, following, evac, t, ada_nb=None):
            for j in range(4):
                if j < 3:
                    nxt = (c4, use, offs[j + 1], j + 1)
                else:
                    nxt = following
                if nxt is not None:
                    for h in range(2):
                        hi_half(*nxt, h)
                if j == 3 and ada_nb is not None:
                    ada_copy(ada_nb, use, 6)
                wait_chunk(act, c4, j)
                evac(c4, j, t)

        def freed(ins, j):
            ins.then_inc(bank_free[j % 2], 1)

        def after_super(sb):
            return (sb + 1, super_use(sb + 1), SUPER[0], 0)

        square_all(x, x_loaded, lambda g: 16)
        root(bank[5][:, 0:T], 1, KT)
        with act.Fori(0, ADA_FIRST) as nb:
            ada_copy(nb, nb, 3)
        for h in range(2):
            hi_half(0, super_use(0), SUPER[0], 0, h)

        def hi_of_h(turn):
            for g in range(4):
                act.wait_ge(prompt_mod, 4 * turn + g + 1)
                act.wait_ge(sample_mod, 4 * turn + g + 1)
                act.activation(h_hi[:, 4 * g:4 * g + 4, :], normed[:, 4 * g:4 * g + 4, :], ACT.Copy).then_inc(h_hi_s, 1)

        hi_of_h(0)

        def evac_v(c4, j, t):
            freed(act.activation(v_cm[:, ds(4 * t + j, 1), :].rearrange("p a t -> p (a t)"), bank[j % 2][:, 0:T],
                                 ACT.Copy), j)

        with act.Fori(0, SB_V) as sb:
            block4(sb, super_use(sb), SUPER, after_super(sb), evac_v, sb, ADA_FIRST + sb)
        for t in range(6):
            act.wait_ge(vt_turned, t + 1)
            tile, half = t // 2, t % 2
            if tile < 2:
                dst, src = v_rows[:, tile, half * 512:half * 512 + 512], bank[6 + t % 2][:, :]
            else:
                dst, src = v_new[:, half * 512:half * 512 + 512], bank[6 + t % 2][0:NS, :]
            act.activation(dst, src, ACT.Copy).then_inc(vt_evac, 1)

        def evac_qk(c4, j, t):
            act.wait_ge(roped, 4 * t + (j + 1))
            freed(act.activation(rope[0][:, :], bank[j % 2][:, 0:T], ACT.Copy), j)

        with act.Fori(0, SB_QK) as t:
            sb = SB_V + t
            block4(sb, super_use(sb), SUPER, after_super(sb), evac_qk, t, ADA_FIRST + sb)

        U0 = SB_V + SB_QK

        def evac_u(n):
            wait_chunk(act, U0, n)
            if n == 0:
                act.wait_ge(hist_set, 1)
            act.activation(u_p[:, n, HIST:UP], bank[n % 2][:, 0:NP_], ACT.Copy)
            freed(act.activation(u_s[:, n, HIST * SEQS:US], bank[n % 2][:, NP_:T], ACT.Copy), n)

        for h in range(HEADS):
            n = h // 2 + 1
            hi_half(U0 + n // 4, super_use(U0 + n // 4), SUPER[n % 4], n % 4, h % 2)
            act.wait_ge(negmax, h + 1)
            if h:
                act.wait_ge(t_done, h)
            for m in range(2):
                for qt in range(2):
                    col, width = (0, 128) if qt == 0 else (128, 256)
                    e = act.activation(probs[:, m, col:col + width], bank[5 + m][:, col:col + width], ACT.Exp,
                                       bias=nb4[:, 2 * m + qt:2 * m + qt + 1], scale=SCALE,
                                       accum_out=sums[:, 2 * m + qt:2 * m + qt + 1])
            e.then_inc(exped, 1)
            if h == 7:
                ada_copy(ADA_FIRST + U0, super_use(U0), 6)
            act.wait_ge(t_done, h + 1)
            if h:
                act.wait_ge(pv_done, h)
            act.activation(probs_t[:, :], bank[7][:, 0:384], ACT.Copy).then_inc(at_ready, 1)
            if h % 2:
                evac_u(h // 2)
            act.wait_ge(pv_done, h + 1)
            act.activation(q_cm[:, h, 0:NP_], bank[3][:, 0:NP_], ACT.Copy).then_inc(o_done, 1)

        for pr in range(4):
            n = 5 + pr
            sb, j = (U0 + n // 4, n % 4)
            for h in range(2):
                hi_half(sb, super_use(sb), SUPER[j], j, h)
            act.wait_ge(dnegmax, pr + 1)
            if pr:
                act.wait_ge(dt_done, pr)
            else:
                act.wait_ge(pv_done, HEADS)
            for t in range(2):
                e = act.activation(dprobs[:, t, :], bank[5 + t][:, 0:T], ACT.Exp, bias=nb4[:, t:t + 1], scale=SCALE,
                                   accum_out=sums[:, t:t + 1])
            e.then_inc(dexped, 1)
            if pr == 3:
                ada_copy(ADA_FIRST + U0 + 1, super_use(U0 + 1), 6)
            evac_u(4 + pr)

        act.wait_ge(dall_done, 1)
        act.activation(q_cm[:, :, NP_:T], bank[7][:, :].rearrange("p (h t) -> p h t", t=NS), ACT.Copy).then_inc(attn_raw, 1)
        act.wait_ge(k_stored, 16)
        act.wait_ge(attn_raw, 1)
        for n in range(5):
            act.activation(sub_sq[:, n * 512:(n + 1) * 512],
                           q_cm[:, :, :].rearrange("p h t -> p (h t)")[:, n * 512:(n + 1) * 512],
                           ACT.Square).then_inc(sub_squared, 1)
        for n in range(5):
            act.wait_ge(sub_mean, n + 1)
            act.activation(sub_sq[:, n * 512:(n + 1) * 512], bank[(3, 5, 6)[n % 3]][:, :], ACT.Sqrt, bias=eps).then_inc(
                sub_root, 1)
        for n in range(5):
            act.wait_ge(sub_scaled, n + 1)
            act.activation(m_hi[:, 0:HEADS, :].rearrange("p h t -> p (h t)")[:, n * 512:(n + 1) * 512],
                           q_cm[:, :, :].rearrange("p h t -> p (h t)")[:, n * 512:(n + 1) * 512], ACT.Copy).then_inc(sub_hi, 1)
        for n in range(8):
            act.wait_ge(y_done, n + 1)
            if n >= 2:
                act.wait_ge(pooled_ready, n - 1)
            act.activation(pool_y[:, n % 2, :], bank[(4, 7)[n % 2]][:, 0:T], ACT.Copy,
                           scale=gain[:, G_POOL + n:G_POOL + n + 1]).then_inc(y_scaled, 1)

        OUT0 = U0 + SB_U

        def evac_out(c4, j, t):
            n = 4 * t + j
            act.activation(back[:, ds(n, 1), :].rearrange("p a t -> p (a t)"), bank[j % 2][:, 0:T], ACT.Copy)
            act.wait_ge(sq_summed, 4 * t + (j + 1))
            freed(act.activation(out_sq[j % 2][:, :], bank[j % 2][:, 0:T], ACT.Square), j)

        def ffn_first(g):
            return (FFN_C4 + 8 * g, ffn_use(g), SUPER[0], 0)

        with act.Fori(0, SB_OUT - 1) as t:
            sb = OUT0 + t
            block4(sb, super_use(sb), SUPER, after_super(sb), evac_out, t, ADA_FIRST + sb)
        block4(N_SB - 1, super_use(N_SB - 1), SUPER, ffn_first(0), evac_out, SB_OUT - 1, ADA_FIRST + N_SB - 1)

        root(bank[5][:, 0:T], 2, KT)
        for g in range(4):
            act.wait_ge(prompt_res, g + 1)
            act.wait_ge(sample_res, g + 1)
            act.activation(squares[:, 4 * g:4 * g + 4, :], x[:, 4 * g:4 * g + 4, :], ACT.Square).then_inc(squared, 1)
        root(bank[5][:, 0:T], 3, KT)
        hi_of_h(1)

        def evac_ff1(g, c4, j, t):
            act.wait_ge(hidden, 16 * g + 4 * t + (j + 1))
            freed(act.activation(relu[j % 2][:, :], bank[j % 2][:, 0:T], ACT.Relu), j)

        def hi_only(c4, use, following):
            for j in range(4):
                nxt = (c4, use, PLAIN[j + 1], j + 1) if j < 3 else following
                if nxt is not None:
                    for h in range(2):
                        hi_half(*nxt, h)

        def mlp_group(g, last):
            c4, use = FFN_C4 + 8 * g, ffn_use(g)
            block4(c4, use, SUPER, (c4 + 1, use + 2, 0, 0), lambda c, j, t: evac_ff1(g, c, j, t), 0,
                   ADA_FIRST + N_SB + g)
            with act.Fori(0, 3) as t:
                block4(c4 + 1 + t, use + 2 + t, PLAIN, (c4 + 2 + t, use + 3 + t, 0, 0),
                       lambda c, j, n: evac_ff1(g, c, j, n), t + 1)
            with act.Fori(0, 3) as t:
                hi_only(c4 + 4 + t, use + 5 + t, (c4 + 5 + t, use + 6 + t, 0, 0))
            hi_only(c4 + 7, use + 8, None if last else ffn_first(g + 1))

        with act.Fori(0, GROUPS - 1) as g:
            mlp_group(g, False)
        mlp_group(GROUPS - 1, True)

        for g in range(4):
            wait_chunk(act, FFN_C4 + 8 * GROUPS - 4 + g, 3)
            act.wait_ge(bank_free[1], 1 + 2 * (FFN_C4 + 8 * GROUPS - 4 + g) + 2)
            act.activation(last_squares[:, 4 * g:4 * g + 4, :], back[:, 4 * g:4 * g + 4, :], ACT.Square).then_inc(squared, 1)
        root(bank[5][:, 0:T], 4, KT)

    @block.vector
    def _(dve):
        mine = Steps(dve, dstep)
        dve.memset(ADA[:, :], 0.0).then_inc(slot_used[0], 2)
        dve.memset(ones[:, :], 1.0 / P).then_inc(ones_set, 1)
        mine.mark(dve.memset(eps, EPS))
        mine.mark(dve.memset(coef4, 1.0))
        for n, (sem, by) in enumerate([(slot_used[1], 2), (slot_used[2], 2), (slot_used[3], 2), (half_free, 4), (bank_free[0], 1),
                                       (bank_free[1], 1), (ada_copied, 1), (sel_done, 1), (mod_done, 1), (roped, 1),
                                       (sq_summed, 2), (hidden, 2)]):
            dve.memset(small[:, 32 + n:33 + n], float(n)).then_inc(sem, by)
        dve.wait_ge(c_exped, 1)
        mine.then(dve.tensor_scalar(c_exp[:, :, :], c_exp[:, :, :], 1.0, None, ALU.add))
        mine.then(dve.reciprocal(c_exp[:, :, :], c_exp[:, :, :]))
        dve.tensor_tensor(silu_c[:, :, :], silu_c[:, :, :], c_exp[:, :, :], ALU.mult).then_inc(silu_done, 1)
        dve.wait_ge(tables_loaded, 80)
        dve.tensor_tensor(lam_pr[:, :], lam_in[:, 0:2], lam_in[:, 2:4], ALU.mult).then_inc(lam_pred, 1)
        dve.wait_ge(lam_exped, 1)
        mine.then(dve.tensor_tensor(small[:, 26:27], lam_e[:, 0:1], lam_e[:, 1:2], ALU.subtract))
        mine.then(dve.tensor_scalar(small[:, 27:28], small[:, 26:27], LAM_INIT, -1.0, ALU.add, ALU.mult))
        mine.mark(dve.tensor_scalar(coef4[:, 2:4], coef4[:, 2:4], small[:, 27:28], None, ALU.mult))
        mine.then(dve.scalar_tensor_tensor(coefd, tab[:, C_M1:C_M1 + 1], small[:, 27:28], tab[:, C_M0:C_M0 + 1],
                                           ALU.mult, ALU.add))
        mine.mark(dve.tensor_scalar(gain[:, G_SUB:G_SUB + 1], gain[:, G_SUB:G_SUB + 1], 1.0 - LAM_INIT, None, ALU.mult))

        def invert_root(turn):
            dve.wait_ge(rooted, turn + 1)
            dve.reciprocal(rstd[:, :], rstd[:, :]).then_inc(rstd_s, 1)
            dve.wait_ge(rstd_s, turn + 1)

        def times_rstd(dst, src, g):
            return dve.tensor_tensor(dst[:, 4 * g:4 * g + 4, :], src[:, 4 * g:4 * g + 4, :],
                                     rstd[:, :].unsqueeze(1).to_broadcast([P, 4, T]), ALU.mult)

        def mod_add(nb):
            dve.wait_ge(sel_done, nb + 2)
            dve.tensor_tensor(mod[:, ds(nb, 1), :, :].rearrange("p a t s -> p (a t) s"),
                              MODT[:, 0:64].rearrange("p (t s) -> p t s", s=16)[:, :, 0:NSEQ],
                              ada_bias[:, ds(nb, 1), :].rearrange("p a t -> p (a t)").unsqueeze(2).to_broadcast(
                                  [P, 4, NSEQ]), ALU.add).then_inc(mod_done, 1)

        def lo_half(c4, use, off, j, h):
            slot, u = use_of(use, off)
            dve.wait_ge(hi_ready, 8 * c4 + (2 * j + h + 1))
            q = 2 * (j % 2) + h
            dve.tensor_tensor(w_lo[q][:, :], raw[slot][:, h * 1024:(h + 1) * 1024], w_hi[q][:, :],
                              ALU.subtract).then_inc(slot_used[slot], 1)

        def block4(c4, use, offs, following, evac, t, ada_nb=None):
            for j in range(4):
                nxt = (c4, use, offs[j + 1], j + 1) if j < 3 else following
                if nxt is not None:
                    for h in range(2):
                        lo_half(*nxt, h)
                evac(c4, j, t)
            if ada_nb is not None:
                mod_add(ada_nb)

        def after_super(sb):
            return (sb + 1, super_use(sb + 1), SUPER[0], 0)

        def wait_evac(c4, j):
            dve.wait_ge(bank_free[j % 2], 2 * c4 + (j // 2 + 2))

        invert_root(0)
        for g in range(4):
            times_rstd(normed, x, g).then_inc(normed_s, 1)
        with dve.Fori(0, ADA_FIRST) as nb:
            mod_add(nb)

        def scale_gain(first_block, g0):
            dve.scalar_tensor_tensor(gate[:, :, :], mod_of(first_block), 1.0,
                                     gain[:, g0:g0 + KT].unsqueeze(2).to_broadcast([P, KT, NSEQ]),
                                     ALU.add, ALU.mult).then_inc(gate_done, 1)

        def gate_gain(first_block, g0):
            dve.tensor_tensor(gate[:, :, :], mod_of(first_block), gain[:, g0:g0 + KT].unsqueeze(2).to_broadcast(
                [P, KT, NSEQ]), ALU.mult).then_inc(gate_done, 1)

        def modulate(turn, shift_block):
            shift = mod_of(shift_block)
            for g in range(4):
                dve.wait_ge(normed_s, 4 * turn + g + 1)
                for k in range(4 * g, 4 * g + 4):
                    last = dve.tensor_scalar(normed[:, k, 0:NP_], normed[:, k, 0:NP_], gate[:, k, 0:1], shift[:, k, 0:1],
                                             ALU.mult, ALU.add)
                last.then_inc(prompt_mod, 1)
            for g in range(4):
                dve.wait_ge(h_hi_s, 4 * turn + g + 1)
                dve.tensor_tensor(h_lo[:, 4 * g:4 * g + 4, :], normed[:, 4 * g:4 * g + 4, :], h_hi[:, 4 * g:4 * g + 4, :],
                                  ALU.subtract).then_inc(h_ready, 1)

        dve.wait_ge(mod_done, ADA_FIRST + 1)
        scale_gain(0, G_PRE_MIX)
        dve.wait_ge(gate_done, 1)
        for h in range(2):
            lo_half(0, super_use(0), SUPER[0], 0, h)
        modulate(0, 4)

        def evac_nothing(c4, j, t):
            pass

        with dve.Fori(0, SB_V) as sb:
            block4(sb, super_use(sb), SUPER, after_super(sb), evac_nothing, sb, ADA_FIRST + sb)

        swap = list(range(8, 16)) + list(range(8)) + list(range(16, 32))

        def evac_qk(c4, j, t):
            wait_evac(c4, j)
            n = 4 * t + j
            mine.mark(dve.tensor_tensor(rope[2][:, :], rope[0][:, :], cos_sin[:, 0, :], ALU.mult))
            mine.mark(dve.stream_shuffle(rope[1][:, :], rope[0][:, :], swap))
            mine.wait()
            mine.then(dve.tensor_tensor(rope[3][:, :], rope[1][:, :], cos_sin[:, 1, :], ALU.mult))
            dve.tensor_tensor(back[:, ds(n, 1), :].rearrange("p a t -> p (a t)"), rope[2][:, :], rope[3][:, :],
                              ALU.add).then_inc(roped, 1)

        with dve.Fori(0, SB_QK) as t:
            sb = SB_V + t
            mine.enter(t, 12)
            block4(sb, super_use(sb), SUPER, after_super(sb), evac_qk, t, ADA_FIRST + sb)
        mine.leave(SB_QK)

        U0 = SB_V + SB_QK
        for h in range(HEADS):
            dve.wait_ge(s_done, h + 1)
            for m in range(2):
                blocks = bank[5 + m][:, 0:512].rearrange("p (s a k) -> p s a k", s=2, a=2)[:, :, 0, :]
                mine.mark(dve.tensor_tensor(blocks, blocks,
                                            tab[:, C_DIAG:C_DIAG + P].unsqueeze(1).to_broadcast([P, 2, P]), ALU.add))
            mine.wait()
            for m in range(2):
                mine.mark(dve.tensor_reduce(nmax[:, 2 * m:2 * m + 1], bank[5 + m][:, 0:128], AX.X, ALU.max, negate=True))
                mine.mark(dve.tensor_reduce(nmax[:, 2 * m + 1:2 * m + 2], bank[5 + m][:, 128:384], AX.X, ALU.max, negate=True))
            mine.wait()
            dve.tensor_scalar(nb4, nmax, SCALE, None, ALU.mult).then_inc(negmax, 1)
            n = h // 2 + 1
            lo_half(U0 + n // 4, super_use(U0 + n // 4), SUPER[n % 4], n % 4, h % 2)
            dve.wait_ge(exped, h + 1)
            mine.then(dve.reciprocal(rsum, sums))
            mine.then(dve.tensor_tensor(rsum, rsum, coef4, ALU.mult))
            for qt in range(2):
                col, width = (0, 128) if qt == 0 else (128, 256)
                mine.mark(dve.tensor_scalar(probs[:, 0, col:col + width], probs[:, 0, col:col + width],
                                            rsum[:, qt:qt + 1], None, ALU.mult))
            mine.wait()
            for qt in range(2):
                col, width = (0, 128) if qt == 0 else (128, 256)
                last = dve.scalar_tensor_tensor(probs[:, 0, col:col + width], probs[:, 1, col:col + width],
                                                rsum[:, 2 + qt:3 + qt], probs[:, 0, col:col + width], ALU.mult, ALU.add)
            last.then_inc(a_ready, 1)
            if h == 7:
                mod_add(ADA_FIRST + U0)

        for pr in range(4):
            dve.wait_ge(ds_done, pr + 1)
            for t in range(2):
                mine.mark(dve.tensor_tensor(bank[5 + t][:, PAST:T], bank[5 + t][:, PAST:T],
                                            tab[:, C_NEWMASK + pr * NS:C_NEWMASK + (pr + 1) * NS], ALU.add))
            mine.wait()
            for t in range(2):
                mine.mark(dve.tensor_reduce(nmax[:, t:t + 1], bank[5 + t][:, 0:T], AX.X, ALU.max, negate=True))
            mine.wait()
            dve.tensor_scalar(nb4[:, 0:2], nmax[:, 0:2], SCALE, None, ALU.mult).then_inc(dnegmax, 1)
            n = 5 + pr
            for h in range(2):
                lo_half(U0 + n // 4, super_use(U0 + n // 4), SUPER[n % 4], n % 4, h)
            dve.wait_ge(dexped, pr + 1)
            mine.then(dve.reciprocal(rsum[:, 0:2], sums[:, 0:2]))
            mine.then(dve.tensor_scalar(rsum[:, 0:2], rsum[:, 0:2], coefd, None, ALU.mult))
            for t in range(2):
                last = dve.tensor_scalar(dprobs[:, t, :], dprobs[:, t, :], rsum[:, t:t + 1], None, ALU.mult)
            last.then_inc(da_ready, 1)
            dve.wait_ge(dt_done, pr + 1)
            if pr:
                dve.wait_ge(dpv_done, pr)
            for t in range(2):
                dve.tensor_copy(dprobs_t[:, t, :, :].rearrange("p a c -> p (a c)"), bank[5 + t][:, T:T + 128])
                last = dve.tensor_copy(
                    dnew_t[:, 4 * t:4 * t + 4, :].rearrange("k h (q b) -> k h b q", b=SEQS)[:, :, 2 * pr:2 * pr + 2, :],
                    bank[5 + t][0:NS, T + 128:512].rearrange("k (h b q) -> k h b q", b=2, q=STEPS))
            last.then_inc(dat_ready, 1)
            if pr == 3:
                mod_add(ADA_FIRST + U0 + 1)

        flat = q_cm[:, :, :].rearrange("p h t -> p (h t)")
        for n in range(5):
            piece = slice(n * 512, (n + 1) * 512)
            dve.wait_ge(sub_root, n + 1)
            mine.then(dve.reciprocal(sub_sq[:, piece], sub_sq[:, piece]))
            dve.scalar_tensor_tensor(flat[:, piece], flat[:, piece], gain[:, G_SUB:G_SUB + 1], sub_sq[:, piece],
                                     ALU.mult, ALU.mult).then_inc(sub_scaled, 1)
        for n in range(5):
            piece = slice(n * 512, (n + 1) * 512)
            dve.wait_ge(sub_hi, n + 1)
            dve.tensor_tensor(m_lo[:, 0:HEADS, :].rearrange("p h t -> p (h t)")[:, piece], flat[:, piece],
                              m_hi[:, 0:HEADS, :].rearrange("p h t -> p (h t)")[:, piece],
                              ALU.subtract).then_inc(attn_ready, 1)
        for n in range(8):
            dve.wait_ge(y_scaled, n + 1)
            mine.then(dve.tensor_copy(m_hi[:, HEADS + n, :], pool_y[:, n % 2, :]))
            dve.tensor_tensor(m_lo[:, HEADS + n, :], pool_y[:, n % 2, :], m_hi[:, HEADS + n, :],
                              ALU.subtract).then_inc(pooled_ready, 1)

        OUT0 = U0 + SB_U
        mine.then(dve.memset(sq_sum[:, :], 0.0))

        def evac_out(c4, j, t):
            wait_evac(c4, j)
            n = 4 * t + j
            dve.tensor_tensor(sq_sum[:, :], sq_sum[:, :], out_sq[j % 2][:, :], ALU.add).then_inc(sq_summed, 1)
            dve.wait_ge(sq_summed, 4 * t + (j + 3))

        def ffn_first(g):
            return (FFN_C4 + 8 * g, ffn_use(g), SUPER[0], 0)

        with dve.Fori(0, SB_OUT - 1) as t:
            sb = OUT0 + t
            block4(sb, super_use(sb), SUPER, after_super(sb), evac_out, t, ADA_FIRST + sb)
        block4(N_SB - 1, super_use(N_SB - 1), SUPER, ffn_first(0), evac_out, SB_OUT - 1, ADA_FIRST + N_SB - 1)

        def residual(turn, root_turn, before):
            invert_root(root_turn)
            for g in range(4):
                times_rstd(back, back, g).then_inc(back_scaled, 1)
                dve.wait_ge(back_scaled, 4 * turn + g + 1)
                for k in range(4 * g, 4 * g + 4):
                    last = dve.scalar_tensor_tensor(x[:, k, 0:NP_], back[:, k, 0:NP_], gate[:, k, 0:1], x[:, k, 0:NP_],
                                                    ALU.mult, ALU.add)
                last.then_inc(prompt_res, 1)

        dve.wait_ge(mod_done, ADA_FIRST + N_SB + 1)
        gate_gain(GATE1, G_POST_MIX)
        dve.wait_ge(gate_done, 2)
        dve.wait_ge(x_again, 16)
        residual(0, 1, None)
        invert_root(2)
        for g in range(4):
            times_rstd(normed, x, g).then_inc(normed_s, 1)
        dve.wait_ge(sample_res, 4)
        scale_gain(SCALE2, G_PRE_FFN)
        dve.wait_ge(gate_done, 3)
        modulate(1, SHIFT2)
        mine.then(dve.memset(back[:, :, :], 0.0))

        def evac_ff1(g, c4, j, t):
            n = 4 * t + j
            wait_evac(c4, j)
            mine.then(dve.tensor_tensor(relu2[j % 2][:, :], relu[j % 2][:, :], relu[j % 2][:, :], ALU.mult))
            hi = m_hi[:, ds(n, 1), :].rearrange("p a t -> p (a t)")
            mine.then(dve.tensor_copy(hi, relu2[j % 2][:, :]))
            dve.tensor_tensor(m_lo[:, ds(n, 1), :].rearrange("p a t -> p (a t)"), relu2[j % 2][:, :], hi,
                              ALU.subtract).then_inc(hidden, 1)

        def evac_ff2(c4, j, t):
            n = 4 * t + j
            wait_chunk(dve, c4, j)
            tile = back[:, ds(n, 1), :].rearrange("p a t -> p (a t)")
            dve.tensor_tensor(tile, bank[j % 2][:, 0:T], tile, ALU.add).then_inc(bank_free[j % 2], 1)

        def mlp_group(g, last):
            c4, use = FFN_C4 + 8 * g, ffn_use(g)
            block4(c4, use, SUPER, (c4 + 1, use + 2, 0, 0), lambda c, j, t: evac_ff1(g, c, j, t), 0,
                   ADA_FIRST + N_SB + g)
            with dve.Fori(0, 3) as t:
                mine.enter(t, 8)
                block4(c4 + 1 + t, use + 2 + t, PLAIN, (c4 + 2 + t, use + 3 + t, 0, 0),
                       lambda c, j, n: evac_ff1(g, c, j, n), t + 1)
            mine.leave(3)
            with dve.Fori(0, 3) as t:
                block4(c4 + 4 + t, use + 5 + t, PLAIN, (c4 + 5 + t, use + 6 + t, 0, 0), evac_ff2, t)
            block4(c4 + 7, use + 8, PLAIN, None if last else ffn_first(g + 1), evac_ff2, 3)

        outer = Steps(dve, dstep)
        outer.base, outer.n = mine.base, mine.n
        with dve.Fori(0, GROUPS - 1) as g:
            outer.enter(g, 32)
            mine.base, mine.n = outer.base, 0
            mlp_group(g, False)
        mine.base, mine.n = outer.start + (GROUPS - 1) * 32, 0
        mlp_group(GROUPS - 1, True)

        dve.wait_ge(mod_done, ADA_FIRST + N_SB + GROUPS + 1)
        gate_gain(GATE2, G_POST_FFN)
        dve.wait_ge(gate_done, 4)
        residual(1, 3, None)

    @block.gpsimd
    def _(pool):
        mine = Steps(pool, pstep)
        pool.dma_start(pages_sb[:, :], table_pg).then_inc(pg_loaded, 16)

        def modulate_samples(turn, shift_block, gates):
            pool.wait_ge(gate_done, gates)
            shift = mod_of(shift_block)
            for g in range(4):
                pool.wait_ge(normed_s, 4 * turn + g + 1)
                tiles = slice(4 * g, 4 * g + 4)
                part = seq_view(normed[:, tiles, NP_:T])
                mine.then(pool.tensor_tensor(part, part, bcast_seq(gate[:, tiles, :]), ALU.mult))
                pool.tensor_tensor(part, part, bcast_seq(shift[:, tiles, :]), ALU.add).then_inc(sample_mod, 1)

        modulate_samples(0, 4, 1)
        mine.then(pool.memset(u_p[:, :, 0:HIST], 0.0))
        pool.dma_start(u_s[:, :, 0:HIST * SEQS], state_cm).then_inc(state_loaded, 16)
        pool.wait_ge(state_loaded, 16)
        pool.memset(small[:, 30:31], 0.0).then_inc(hist_set, 1)

        pool.wait_ge(bank_free[0], 2 * SB_V + 1)
        pool.wait_ge(bank_free[1], 2 * SB_V + 1)
        pool.dma_start(v_out, v_cm[:, :, :]).then_inc(v_stored, 16)
        pool.wait_ge(pg_loaded, 16)
        pool.wait_ge(v_stored, 16)
        pool.wait_ge(vt_evac, 6)

        def load_pages(cache, dst, b, sems):
            for pg in range(PAGES):
                n = b * PAGES + pg
                page = pool.value_load(pages_sb[0:1, n:n + 1], min_val=0, max_val=cache.shape[0] - 1)
                pool.dma_start(dst[:, b % 2, pg, :], cache[ds(page, 1), :, :].rearrange("a p n -> p (a n)")).then_inc(
                    sems[b % 2], 16)

        for b in range(2):
            load_pages(kc, k_pages, b, k_loaded)
            load_pages(vc, v_pages, b, v_loaded)
        pool.wait_ge(roped, 17)
        pool.dma_start(k_out, k_cm[:, :, :]).then_inc(k_stored, 16)

        U0 = SB_V + SB_QK

        def pool_tile(n):
            pool.wait_ge(bank_free[n % 2], 2 * U0 + (n // 2 + 2))
            pool.dma_start(poolp_out[:, n, :], u_p[:, n, NP_:UP]).then_inc(pool_stored, 16)
            pool.dma_start(pools_out[:, n, :], u_s[:, n, STEPS * SEQS:US]).then_inc(pool_stored, 16)
            group = n // 2
            src_p, src_s = u_p[:, n, :], u_s[:, n, :]
            for level in range(group + 1):
                back_by, start = 1 << level, (2 << level) - 1
                dst = win[level % 2]
                mine.mark(pool.tensor_tensor(dst[:, start:UP], src_p[:, start:UP], src_p[:, start - back_by:UP - back_by],
                                             ALU.add))
                mine.then(pool.tensor_tensor(dst[:, UP + start * SEQS:UP + US], src_s[:, start * SEQS:US],
                                             src_s[:, (start - back_by) * SEQS:US - back_by * SEQS], ALU.add))
                src_p, src_s = dst[:, 0:UP], dst[:, UP:UP + US]
            mine.then(pool.tensor_tensor(src_p[:, HIST:HIST + 16], src_p[:, HIST:HIST + 16],
                                         tab[:, C_FIX + 16 * group:C_FIX + 16 * group + 16], ALU.mult))
            mine.mark(pool.tensor_scalar(src_p[:, HIST:UP], src_p[:, HIST:UP], 1.0 / (2 << group), 1.0, ALU.mult, ALU.mult))
            mine.then(pool.tensor_scalar(src_s[:, HIST * SEQS:US], src_s[:, HIST * SEQS:US], 1.0 / (2 << group), 1.0,
                                         ALU.mult, ALU.mult))
            pool.wait_ge(pool_stored, 32 * (n + 1))
            pool.tensor_tensor(u_p[:, n, HIST:UP], src_p[:, HIST:UP], u_p[:, n, HIST:UP], ALU.subtract)
            pool.tensor_tensor(u_s[:, n, HIST * SEQS:US], src_s[:, HIST * SEQS:US], u_s[:, n, HIST * SEQS:US],
                               ALU.subtract).then_inc(pooled, 1)
            pool.wait_ge(pooled, n + 1)

        mine.then(pool.memset(q_pick[:, :, :, :], 0.0))
        for n in range(3):
            pool_tile(n)
        for pr in range(4):
            if pr:
                pool.wait_ge(ds_done, pr)
            for par in range(2):
                b = 2 * pr + par
                for m in range(2):
                    rows = slice(m * HD, (m + 1) * HD)
                    pool.tensor_copy(q_pick[rows, par, :, 16 * par + 8 * m:16 * par + 8 * m + 8],
                                     q_cm[rows, :, NP_ + b:T:SEQS]).then_inc(q_ready, 1)
                    pool.wait_ge(q_ready, 4 * pr + 2 * par + m + 1)
            if pr < 3:
                pool.wait_ge(ds_done, pr + 1)
                for b in (2 * pr + 2, 2 * pr + 3):
                    load_pages(kc, k_pages, b, k_loaded)
            pool_tile(3 + pr)
            if pr < 3:
                pool.wait_ge(dpv_done, pr + 1)
                for b in (2 * pr + 2, 2 * pr + 3):
                    load_pages(vc, v_pages, b, v_loaded)
        wait_chunk(pool, U0 + 1, 3)
        pool.dma_start(pool_w[:, :, :, :], w_pool).then_inc(poolw_loaded, 16)
        pool_tile(7)
        pool.wait_ge(y_done, 8)
        pool.wait_ge(dpv_done, 4)
        pool.dma_start(x[:, :, :], x_cm).then_inc(x_again, 16)

        def residual_samples(turn, gates):
            pool.wait_ge(gate_done, gates)
            for g in range(4):
                pool.wait_ge(back_scaled, 4 * turn + g + 1)
                tiles = slice(4 * g, 4 * g + 4)
                part = seq_view(back[:, tiles, NP_:T])
                xs = x[:, tiles, NP_:T]
                mine.then(pool.tensor_tensor(part, part, bcast_seq(gate[:, tiles, :]), ALU.mult))
                pool.tensor_tensor(xs, xs, back[:, tiles, NP_:T], ALU.add).then_inc(sample_res, 1)

        pool.wait_ge(x_again, 16)
        residual_samples(0, 2)
        modulate_samples(1, SHIFT2, 3)
        residual_samples(1, 4)

    @block.tensor
    def _(pe):
        pe.wait_ge(ones_set, 1)
        pe.wait_ge(lam_pred, 1)
        pe.matmul(bank[6][:, 0:2], ones[0:HD, :], lam_pr[:, :], start=True, stop=True).then_inc(lam_summed, 1)

        def mean_squares(turn, one=None, src=squares):
            if one is not None:
                pe.matmul(bank[5][:, 0:T], ones[:, :], one, start=True, stop=True).then_inc(meaned, 1)
                return
            for g in range(4):
                pe.wait_ge(squared, 4 * turn + g + 1)
                for k in range(4 * g, 4 * g + 4):
                    last = pe.matmul(bank[5][:, 0:T], ones[:, :], src[:, k, :], start=(k == 0), stop=(k == KT - 1))
            last.then_inc(meaned, 1)

        mean_squares(0)

        def ada_chunk(nb, use, off, a):
            slot, u = use_of(use, off)
            pe.wait_ge(raw_loaded[slot], 16 * (u + 1))
            if a == 0:
                pe.wait_ge(ada_copied, nb + 1)
            for kk in range(4):
                last = pe.matmul(ADA[32 * kk:32 * kk + NSEQ, :], silu_c[:, 4 * a + kk, :],
                                 raw[slot][:, kk * 512:(kk + 1) * 512], start=(a == 0), stop=(a == 3))
            last.then_inc(slot_used[slot], 2)

        def ada_turn(nb):
            pe.wait_ge(ada_copied, nb + 2)
            pe.wait_ge(mod_done, nb + 1)
            for t in range(4):
                last = pe.matmul(MODT[:, 16 * t:16 * t + NSEQ], ada_rows[:, t * P:(t + 1) * P], tab[:, C_PICK9:C_PICK9 + NSEQ],
                                 start=True, stop=True)
            last.then_inc(sel_done, 1)

        def product_half(c4, use, off, j, h, xh, xl, ready):
            slot, u = use_of(use, off)
            if h == 0:
                pe.wait_ge(bank_free[j % 2], 2 * c4 + (j // 2 + 1))
            ready(h)
            pe.wait_ge(slot_used[slot], 2 * u + (3 + h))
            q = 2 * (j % 2) + h
            for k in range(8):
                for n, (w, v) in enumerate(((w_hi, xh), (w_hi, xl), (w_lo, xh))):
                    last = pe.matmul(bank[j % 2][:, 0:T], w[q][:, k * P:(k + 1) * P], v[:, 8 * h + k, :],
                                     start=(h == 0 and k == 0 and n == 0), stop=(h == 1 and k == 7 and n == 2))
            last.then_inc(half_free, 1)

        def super4(sb_c4, use, nb, xh, xl, ready):
            for j in range(4):
                ada_chunk(nb, use, 2 * j, j)
                for h in range(2):
                    product_half(sb_c4, use, SUPER[j], j, h, xh, xl, ready)
            ada_turn(nb)

        def plain4(c4, use, xh, xl, ready):
            for j in range(4):
                for h in range(2):
                    product_half(c4, use, PLAIN[j], j, h, xh, xl, ready)

        pe.wait_ge(silu_done, 1)
        with pe.Fori(0, ADA_FIRST) as nb:
            for a in range(4):
                ada_chunk(nb, nb, a, a)
            ada_turn(nb)

        def h_wait(turn):
            return lambda h: pe.wait_ge(h_ready, 4 * turn + 2 * h + 2)

        with pe.Fori(0, SB_V) as sb:
            super4(sb, super_use(sb), ADA_FIRST + sb, h_hi, h_lo, h_wait(0))
        pe.wait_ge(bank_free[0], 2 * SB_V + 1)
        pe.wait_ge(bank_free[1], 2 * SB_V + 1)
        for t in range(6):
            tile, half = t // 2, t % 2
            if t >= 2:
                pe.wait_ge(vt_evac, t - 1)
            rows = P if tile < 2 else NS
            for n in range(4):
                last = pe.transpose(bank[6 + t % 2][0:rows, n * P:(n + 1) * P],
                                    v_cm[:, 4 * half + n, tile * P:tile * P + rows], ident)
            last.then_inc(vt_turned, 1)
        with pe.Fori(SB_V, SB_V + SB_QK) as sb:
            super4(sb, super_use(sb), ADA_FIRST + sb, h_hi, h_lo, h_wait(0))

        U0 = SB_V + SB_QK

        def u_half(n, h):
            sb, j = U0 + n // 4, n % 4
            if h == 0:
                ada_chunk(ADA_FIRST + sb, super_use(sb), 2 * j, j)
            product_half(sb, super_use(sb), SUPER[j], j, h, h_hi, h_lo, h_wait(0))
            if j == 3 and h == 1:
                ada_turn(ADA_FIRST + sb)

        def scores(h):
            if h:
                pe.wait_ge(exped, h)
            else:
                pe.wait_ge(roped, 17)
                pe.wait_ge(vt_evac, 6)
            for qt in range(2):
                for m in range(2):
                    rows = slice(m * HD, (m + 1) * HD)
                    col, width = (0, 128) if qt == 0 else (128, 256)
                    last = pe.matmul(bank[5 + m][:, col:col + width], q_cm[rows, h, qt * P:(qt + 1) * P],
                                     k_cm[rows, h, 0:width], start=True, stop=True)
            last.then_inc(s_done, 1)

        scores(0)
        for h in range(HEADS):
            u_half(h // 2, h % 2)
            pe.wait_ge(a_ready, h + 1)
            if h:
                pe.wait_ge(at_ready, h)
            for n in range(3):
                last = pe.transpose(bank[7][:, n * P:(n + 1) * P], probs[:, 0, n * P:(n + 1) * P], ident)
            last.then_inc(t_done, 1)
            if h + 1 < HEADS:
                scores(h + 1)
            pe.wait_ge(at_ready, h + 1)
            if h:
                pe.wait_ge(o_done, h)
            cols = slice(h * P, (h + 1) * P)
            pe.matmul(bank[3][:, 0:NP_], v_rows[:, 0, cols], probs_t[:, 0:NP_], start=True, stop=False)
            pe.matmul(bank[3][:, P:NP_], v_rows[:, 1, cols], probs_t[:, NP_:384], start=False, stop=True).then_inc(pv_done, 1)

        for pr in range(4):
            pe.wait_ge(q_ready, 4 * (pr + 1))
            if pr:
                pe.wait_ge(dat_ready, pr)
            else:
                pe.wait_ge(exped, HEADS)
            for par in range(2):
                pe.wait_ge(k_loaded[par], 32 * (pr + 1))
                for t in range(2):
                    for part in range(2):
                        for j in range(4):
                            h = 4 * t + j
                            if part == 0:
                                out = bank[5 + t][32 * j:32 * j + 32, 0:PAST]
                                rhs = k_pages[:, par, :, h * PAGE:(h + 1) * PAGE]
                            else:
                                out = bank[5 + t][32 * j:32 * j + 32, PAST:T]
                                rhs = k_cm[:, h, NP_:T]
                            last = pe.matmul(out, q_pick[:, par, h, :], rhs, start=(par == 0 and part == 0),
                                             stop=(par == 1 and part == 1), skip_group_check=True)
            last.then_inc(ds_done, 1)
            for h in range(2):
                u_half(4 + pr, h)
            pe.wait_ge(da_ready, pr + 1)
            for t in range(2):
                pick = tab[:, C_PICK64:C_PICK64 + 64]
                for pg in range(PAGES):
                    pe.matmul(bank[5 + t][:, T + 64 * pg:T + 64 * pg + 64], dprobs[:, t, pg * PAGE:(pg + 1) * PAGE], pick,
                              start=True, stop=True)
                last = pe.matmul(bank[5 + t][0:NS, T + 128:512], dprobs[:, t, PAST:T], pick, start=True, stop=True)
            last.then_inc(dt_done, 1)
            pe.wait_ge(dat_ready, pr + 1)
            if pr == 0:
                pe.wait_ge(at_ready, HEADS)
            outs = bank[7][:, :].rearrange("p (h q b) -> p h q b", h=HEADS, b=SEQS)
            for par in range(2):
                pe.wait_ge(v_loaded[par], 32 * (pr + 1))
                for h in range(HEADS):
                    for pg in range(PAGES):
                        last = pe.matmul(outs[:, h, :, 2 * pr + par], v_pages[:, par, pg, h * P:(h + 1) * P],
                                         dprobs_t[:, h // 4, pg, 16 * (h % 4) + 8 * par:16 * (h % 4) + 8 * par + 8],
                                         start=(pr == 0 and par == 0 and h == 0 and pg == 0), stop=False,
                                         skip_group_check=True)
            last.then_inc(dpv_done, 1)
        for h in range(HEADS):
            last = pe.matmul(bank[7][:, h * NS:(h + 1) * NS], v_new[:, h * P:(h + 1) * P], dnew_t[:, h, :],
                             start=False, stop=(h == HEADS - 1), skip_group_check=True)
        last.then_inc(dall_done, 1)

        for n in range(5):
            pe.wait_ge(sub_squared, n + 1)
            if n >= 3:
                pe.wait_ge(sub_root, n - 2)
            elif n == 0:
                pe.wait_ge(o_done, HEADS)
            pe.matmul(bank[(3, 5, 6)[n % 3]][:, :], ones[:, :], sub_sq[:, n * 512:(n + 1) * 512], start=True,
                      stop=True).then_inc(sub_mean, 1)
        pe.wait_ge(poolw_loaded, 16)
        pe.wait_ge(pooled, 8)
        pe.wait_ge(attn_raw, 1)
        pe.wait_ge(mod_done, ADA_FIRST + U0 + 3)
        for n in range(8):
            g, half = n // 2, n % 2
            if n >= 2:
                pe.wait_ge(y_scaled, n - 1)
            out = bank[(4, 7)[n % 2]]
            for k in range(2):
                w = pool_w[:, g, k, half * P:(half + 1) * P]
                pe.matmul(out[:, 0:NP_], w, u_p[:, 2 * g + k, HIST:UP], start=(k == 0), stop=False, skip_group_check=True)
                last = pe.matmul(out[:, NP_:T], w, u_s[:, 2 * g + k, HIST * SEQS:US], start=False, stop=(k == 1),
                                 skip_group_check=True)
            last.then_inc(y_done, 1)

        OUT0 = U0 + SB_U

        def mix_wait(h):
            if h == 0:
                pe.wait_ge(attn_ready, 5)
            else:
                pe.wait_ge(pooled_ready, 8)

        with pe.Fori(OUT0, OUT0 + SB_OUT) as sb:
            super4(sb, super_use(sb), ADA_FIRST + sb, m_hi, m_lo, mix_wait)
        pe.wait_ge(sq_summed, 2 + KT)
        mean_squares(1, sq_sum[:, :])
        mean_squares(1)

        def hidden_wait(g):
            return lambda h: pe.wait_ge(hidden, 16 * g + (2 + 8 * h + 8))

        with pe.Fori(0, GROUPS) as g:
            c4, use = FFN_C4 + 8 * g, ffn_use(g)
            super4(c4, use, ADA_FIRST + N_SB + g, h_hi, h_lo, h_wait(1))
            with pe.Fori(0, 3) as t:
                plain4(c4 + 1 + t, use + 2 + t, h_hi, h_lo, h_wait(1))
            with pe.Fori(0, 4) as t:
                plain4(c4 + 4 + t, use + 5 + t, m_hi, m_lo, hidden_wait(g))
        mean_squares(2, src=last_squares)

    block.__exit__(None, None, None)


def shape_tables():
    tab = np.zeros((P, C_END), np.float32)
    rows = np.arange(P)
    tab[:, C_ID:C_ID + P] = np.eye(P)
    tab[:, C_DIAG:C_DIAG + P] = np.where(rows[None, :] <= rows[:, None], 0.0, MASKED)
    par, m, q = rows // 16 % 2, rows // 8 % 2, rows % 8
    key_q, key_b = np.arange(NS) // SEQS, np.arange(NS) % SEQS
    for pr in range(4):
        seen = (key_b[None, :] == 2 * pr + par[:, None]) & (key_q[None, :] <= q[:, None])
        tab[:, C_NEWMASK + pr * NS:C_NEWMASK + (pr + 1) * NS] = np.where(seen, 0.0, MASKED)
    for s in range(NSEQ):
        tab[s::32, C_PICK9 + s] = 1.0
    tab[rows, C_PICK64 + rows // 32 * 16 + par * 8 + q] = 1.0
    tab[:, C_M0], tab[:, C_M1] = m == 0, m == 1
    for g in range(POOL_GROUPS):
        w = 2 << g
        tab[:, C_FIX + 16 * g:C_FIX + 16 * g + 16] = w / np.minimum(w, np.arange(16) + 1)
    rot = HD // 4
    inv = (np.float32(1.0) / np.float32(500000.0) ** (np.arange(0, rot, 2, dtype=np.float32) / np.float32(rot))).astype(np.float32)
    pos = np.concatenate([np.arange(NP_), PAST + np.repeat(np.arange(STEPS), SEQS)]).astype(np.float32)
    trig = np.zeros((P, 2, T), np.float32)
    trig[:, 0] = 1.0
    for p in range(P):
        d = p % HD
        if d < rot:
            ang = (pos * inv[d % (rot // 2)]).astype(np.float32)
            trig[p, 0] = np.cos(ang)
            trig[p, 1] = np.sin(ang) * (-1.0 if d < rot // 2 else 1.0)
    return tab, trig


def weight_stream(w_ada, w_in, w_out, w_ff1, w_ff2):
    def ada_block(nb):
        first = [1, 0, 2, 4, 3, 5][nb // 4] * D + nb % 4 * 512
        part = w_ada[:, first:first + 512].reshape(4, 4, P, 512)
        return [part[a].transpose(1, 0, 2).reshape(P, 2048) for a in range(4)]

    def chunk(w, col, row=0):
        return w[row:row + D, col * P:(col + 1) * P].reshape(KT, P, P).transpose(1, 0, 2).reshape(P, 2048)

    first_v, first_q, first_u = 16, 0, 24
    order = [first_v + n for n in range(8)] + [first_q + n for n in range(16)] + [first_u + n for n in range(8)]
    chunks = [c for nb in range(ADA_FIRST) for c in ada_block(nb)]
    mains = [chunk(w_in, n) for n in order] + [chunk(w_out, n) for n in range(16)]

    def superblock(nb, four):
        return [c for a, m in zip(ada_block(nb), four) for c in (a, m)]

    for sb in range(SB_V + SB_QK + SB_U + SB_OUT):
        chunks += superblock(ADA_FIRST + sb, mains[4 * sb:4 * sb + 4])
    for g in range(GROUPS):
        up = [chunk(w_ff1, 16 * g + n) for n in range(16)]
        chunks += superblock(20 + g, up[:4]) + up[4:] + [chunk(w_ff2, n, g * D) for n in range(16)]
    assert len(chunks) == STREAM
    return np.stack(chunks)


def channel_major(rows):
    return np.ascontiguousarray(rows.reshape(rows.shape[0], -1, P).transpose(2, 1, 0))


def kernel(**inputs):
    import concourse.bacc as bacc
    from concourse.bass_utils import run_bass_kernel_spmd

    a = {k: np.asarray(v) for k, v in inputs.items()}
    xs = a["x_sample"].transpose(1, 0, 2).reshape(NS, D)
    tab, trig = shape_tables()
    n_phys = a["cache_k"].shape[1]
    arrays = {
        "stream": weight_stream(a["w_ada"][0], a["w_in"][0], a["w_out"][0], a["w_ff1"][0], a["w_ff2"][0]),
        "x_cm": channel_major(np.concatenate([a["x_prompt"][0], xs])),
        "c_cm": channel_major(np.concatenate([a["c_prompt"], a["c_sample"]])),
        "kc": np.ascontiguousarray(a["cache_k"][0].transpose(0, 3, 2, 1)).reshape(n_phys, P, HEADS * PAGE),
        "vc": a["cache_v"][0].reshape(n_phys, PAGE, HEADS * P),
        "table_pg": a["page_table"].reshape(1, SEQS * PAGES),
        "state_cm": np.ascontiguousarray(a["state_pool"][0].reshape(SEQS, HIST, 8, P).transpose(3, 2, 1, 0)).reshape(
            P, 8, HIST * SEQS),
        "w_pool": np.ascontiguousarray(a["w_pool"][0].reshape(POOL_GROUPS, 2, P, 256).transpose(2, 0, 1, 3)),
        "bias": np.ascontiguousarray(a["b_ada"][0].reshape(6, 4, 4, P)[[1, 0, 2, 4, 3, 5]].reshape(24, 4, P).transpose(2, 0, 1)),
        "gains": np.ascontiguousarray(np.concatenate(
            [a[n][0].reshape(-1, P) for n in ("g_pre_mix", "g_post_mix", "g_pre_ffn", "g_post_ffn", "pool_scale", "g_subln")]).T),
        "lam4": np.ascontiguousarray(np.stack([a[n][0] for n in ("lambda_q1", "lambda_q2", "lambda_k1", "lambda_k2")], 1)),
        "trig": trig,
        "consts": tab,
    }
    outs = {"y_out": (P, KT, T), "k_out": (P, HEADS, T), "v_out": (P, HEADS, T), "poolp_out": (P, 8, HIST),
            "pools_out": (P, 8, HIST * SEQS)}
    nc = bacc.Bacc("TRN2", target_bir_lowering=False, num_devices=1)
    args = [nc.dram_tensor("in_" + n, v.shape, mybir.dt.from_np(v.dtype), kind="ExternalInput").ap() for n, v in arrays.items()]
    args += [nc.dram_tensor(n, s, mybir.dt.float32, kind="ExternalOutput").ap() for n, s in outs.items()]
    decoder_step(nc, *args)
    got = run_bass_kernel_spmd(nc, [{"in_" + n: v for n, v in arrays.items()}], core_ids=[0]).results[0]

    def rows(cm):
        r = cm.transpose(2, 1, 0).reshape(T, -1)
        return r[:NP_], r[NP_:].reshape(STEPS, SEQS, -1).transpose(1, 0, 2)

    y_p, y_s = rows(got["y_out"])
    k_p, k_s = rows(got["k_out"])
    v_p, v_s = rows(got["v_out"])
    pool_p = got["poolp_out"].transpose(2, 1, 0).reshape(1, 1, HIST, 8 * P)
    pool_s = got["pools_out"].reshape(P, 8, HIST, SEQS).transpose(3, 2, 1, 0).reshape(1, SEQS, HIST, 8 * P)
    return (y_p[None], y_s, k_p.reshape(1, 1, NP_, HEADS, P), v_p.reshape(1, 1, NP_, HEADS, P), pool_p,
            k_s.reshape(1, SEQS, STEPS, HEADS, P), v_s.reshape(1, SEQS, STEPS, HEADS, P), pool_s)
```

```python
import concourse.bass as bass
from concourse import mybir
import numpy as np

P = 128
D = 2048
KT = D // P
NP_, NS = 256, 64
T = NP_ + NS
SEQS, STEPS = 8, 8
NSEQ = 1 + SEQS
HEADS, HD = 8, 64
PAST, PAGE, PAGES = 256, 128, 2
HIST = 15
UP = HIST + NP_
US = (HIST + STEPS) * SEQS
POOL_GROUPS = 4
LAM_INIT = 0.8 - 0.6
SCALE = HD ** -0.5
EPS = 1e-6
MASKED = -1e30
GROUPS = 4

QUARTERS, Q_GROUPS, U_GROUPS, OUT_GROUPS = 4, 2, 2, 4
STREAM = 8 + 12 * QUARTERS + 12 * Q_GROUPS + 8 * (U_GROUPS + OUT_GROUPS) + 36 * GROUPS
DENSE = [2, 5, 8, 11]
DENSE_ADA = [[0, 1, 3, 4], [6, 7, 9, 10]]
SUPER = [1, 3, 5, 7]
PLAIN = [0, 1, 2, 3]
Q_C4 = QUARTERS
U_C4 = Q_C4 + Q_GROUPS
OUT_C4 = U_C4 + U_GROUPS
FFN_C4 = OUT_C4 + OUT_GROUPS
BANK_LEAD = 4 * QUARTERS - 2 * Q_C4
PIECES = [("dve", 0, 4), ("pool", 11, 14), ("dve", 4, 8), ("pool", 14, KT), ("dve", 8, 11)]
PAIR_FILLS = [[10, 11], [12, 13], [14], [15]]

C_ID, C_DIAG = 0, 128
C_NEWMASK, C_PICK9 = 256, 512
C_PICK, C_M0, C_M1 = 521, 649, 650
C_FIX, C_END = 651, 715

G_PRE_MIX, G_POST_MIX, G_PRE_FFN, G_POST_FFN, G_POOL, G_SUB, G_END = 0, 16, 32, 48, 64, 72, 73


class Steps:

    def __init__(self, eng, sem):
        self.eng, self.sem, self.base, self.n = eng, sem, 0, 0

    def mark(self, instruction):
        instruction.then_inc(self.sem, 1)
        self.n += 1

    def wait(self):
        self.eng.wait_ge(self.sem, self.base + self.n)

    def then(self, instruction):
        self.mark(instruction)
        self.wait()

    def enter(self, i, per):
        self.start, self.per = self.base + self.n, per
        self.base, self.n = self.start + i * per, 0

    def leave(self, turns):
        assert self.n == self.per, self.n
        self.base, self.n = self.start + turns * self.per, 0


def decoder_step(nc, stream, x_cm, c_cm, kc, vc, table_pg, state_cm, w_pool, bias, gains, lam4, trig, consts,
                 y_out, k_out, v_out, poolp_out, pools_out):
    f32, f32r, i32 = mybir.dt.float32, mybir.dt.float32r, mybir.dt.int32
    ALU, ACT, AX = mybir.AluOpType, mybir.ActivationFunctionType, mybir.AxisListType
    ds = bass.ds

    base = (nc.sbuf_base + 31) // 32 * 32
    cursor = [base]

    def at(name, shape, dtype, offset):
        return nc.alloc_sbuf_tensor_at(name, shape, dtype, offset=offset)

    def region(nbytes):
        start = cursor[0]
        cursor[0] += (nbytes + 31) // 32 * 32
        assert cursor[0] <= nc.sbuf_usable_end, cursor[0]
        return start

    def own(name, shape, dtype=f32):
        return at(name, shape, dtype, region(4 * int(np.prod(shape[1:]))))

    raw = [own(f"raw{s}", [P, 2048]) for s in range(4)]
    w_hi = [own(f"w_hi{q}", [P, 1024], f32r) for q in range(4)]
    w_lo = [own(f"w_lo{q}", [P, 1024], f32r) for q in range(4)]
    R_H = region(2 * KT * T * 4)
    h_hi, h_lo = at("h_hi", [P, KT, T], f32r, R_H), at("h_lo", [P, KT, T], f32r, R_H + KT * T * 4)
    pool_w = at("pool_w", [P, POOL_GROUPS, 2, 256], f32, R_H)
    R_C = region(2 * KT * T * 4)
    m_hi, m_lo = at("m_hi", [P, KT, T], f32r, R_C), at("m_lo", [P, KT, T], f32r, R_C + KT * T * 4)
    v_cm = at("v_cm", [P, HEADS, T], f32, R_C)
    k_pages = at("k_pages", [P, 2, PAGES, HEADS * PAGE], f32, R_C)
    v_pages = at("v_pages", [P, 2, PAGES, HEADS * P], f32, R_C + 16384)
    v_rows = at("v_rows", [P, 2, HEADS * P], f32, R_C + 32768)
    squares = at("squares", [P, KT, T], f32, R_C)
    normed = at("normed", [P, KT, T], f32, R_C + KT * T * 4)
    R_X = region(KT * T * 4)
    x = at("x", [P, KT, T], f32, R_X)
    u_p = at("u_p", [P, HEADS, UP], f32, R_X)
    u_s = at("u_s", [P, HEADS, US], f32, R_X + HEADS * UP * 4)
    R_XS = R_X + HEADS * (UP + US) * 4
    probs = at("probs", [P, 2, 384], f32, R_XS)
    probs_t = at("probs_t", [P, 384], f32, R_XS + 3072)
    dprobs = at("dprobs", [P, 2, PAST + NS], f32, R_XS)
    dprobs_t = at("dprobs_t", [P, 2, PAGES, P], f32, R_XS + 3072)
    R_A = region(KT * T * 4)
    back = at("back", [P, KT, T], f32, R_A)
    q_cm, k_cm = back[:, 0:HEADS, :], back[:, HEADS:KT, :]
    sub_sq = k_cm
    v_new = own("v_new", [NS, HEADS * P])
    ada_rows = own("ada_rows", [P, 512])
    R_S = region(5120)
    rope = [at(f"rope{n}", [P, T], f32, R_S + n * T * 4) for n in range(4)]
    q_pick = at("q_pick", [P, 2, HEADS, 32], f32, R_S)
    dnew_t = at("dnew_t", [NS, 2, P], f32, R_S + 2048)
    d_rows = at("d_rows", [P, 512], f32, R_S + 3072)
    out_sq = [at(f"out_sq{n}", [P, T], f32, R_S + n * T * 4) for n in range(2)]
    sq_sum = at("sq_sum", [P, T], f32, R_S + 2 * T * 4)
    relu = [at(f"relu{n}", [P, T], f32, R_S + n * T * 4) for n in range(2)]
    relu2 = [at(f"relu2{n}", [P, T], f32, R_S + (2 + n) * T * 4) for n in range(2)]
    R_T = region(3 * T * 4)
    cos_sin = at("cos_sin", [P, 2, T], f32, R_T)
    rstd = at("rstd", [P, T], f32, R_T + 2 * T * 4)
    win = [at(f"win{n}", [P, UP + US], f32, R_T + n * 1824) for n in range(2)]
    mod = own("mod", [P, 24, 4, NSEQ])
    gate = own("gate", [P, KT, NSEQ])
    tab = own("tab", [P, C_END])
    gain = own("gain", [P, G_END])
    ada_bias = own("ada_bias", [P, 24, 4])
    ones = own("ones", [P, P])
    silu_c = own("silu_c", [P, KT, NSEQ])
    lam_in = own("lam_in", [HD, 4])
    lam_pr = own("lam_pr", [HD, 2])
    small = own("small", [P, 48])
    pages_sb = own("pages_sb", [1, SEQS * PAGES], i32)

    eps = small[:, 0:1]
    lam_e = small[:, 1:3]
    coef4 = small[:, 3:7]
    coefd = small[:, 7:8]
    nmax, nb4, sums, rsum = small[:, 8:12], small[:, 12:16], small[:, 16:20], small[:, 20:24]
    c_exp = at("c_exp", [P, KT, NSEQ], f32, R_S)
    ident = tab[:, C_ID:C_ID + P]
    scr = {"dn": small[:, 24:26]}

    bank = [nc.alloc_psum_tensor(f"bank{n}", [P, 512], f32) for n in range(8)]
    ADA, MODT = bank[2], bank[4]
    QUARTER_BANKS = [bank[0], bank[1], bank[3], bank[7]]

    def S(name):
        return nc.alloc_semaphore(name)

    raw_loaded = [S(f"raw_loaded{s}") for s in range(4)]
    slot_used = [S(f"slot_used{s}") for s in range(4)]
    half_free = S("half_free")
    bank_free = [S(f"bank_free{b}") for b in range(4)]
    first_done = S("first_done")
    hi_ready = S("hi_ready")
    x_loaded, c_loaded, tables_loaded, pg_loaded = S("x_loaded"), S("c_loaded"), S("tables_loaded"), S("pg_loaded")
    lam_loaded, sums_zeroed = S("lam_loaded"), S("sums_zeroed")
    ones_set, c_exped, silu_done, lam_pred, lam_summed, lam_exped = [S(n) for n in (
        "ones_set", "c_exped", "silu_done", "lam_pred", "lam_summed", "lam_exped")]
    squared, meaned, rooted, normed_s, rstd_s = S("squared"), S("meaned"), S("rooted"), S("normed_s"), S("rstd_s")
    ada_copied, sel_done, mod_done = S("ada_copied"), S("sel_done"), S("mod_done")
    gate_done = S("gate_done")
    prompt_mod, sample_mod, h_hi_s, h_ready = S("prompt_mod"), S("sample_mod"), S("h_hi_s"), S("h_ready")
    roped = S("roped")
    dstep, astep, pstep = S("dstep"), S("astep"), S("pstep")
    vt_turned, vt_evac, v_stored, k_stored = S("vt_turned"), S("vt_evac"), S("v_stored"), S("k_stored")
    k_loaded, v_loaded = [S("k_loaded0"), S("k_loaded1")], [S("v_loaded0"), S("v_loaded1")]
    s_done, negmax, exped, a_ready, t_done, at_ready, pv_done, o_done = [S(n) for n in (
        "s_done", "negmax", "exped", "a_ready", "t_done", "at_ready", "pv_done", "o_done")]
    q_ready, ds_done, dnegmax, dexped, da_ready, dt_done, dat_ready, dpv_done = [S(n) for n in (
        "q_ready", "ds_done", "dnegmax", "dexped", "da_ready", "dt_done", "dat_ready", "dpv_done")]
    d_evac, d_turned, d_out = S("d_evac"), S("d_turned"), S("d_out")
    sub_squared, sub_mean, sub_copied, sub_root, sub_scaled, sub_hi, attn_ready = [S(n) for n in (
        "sub_squared", "sub_mean", "sub_copied", "sub_root", "sub_scaled", "sub_hi", "attn_ready")]
    hist_set, state_loaded, pool_stored, pooled, poolw_loaded, y_done, y_hi, pooled_ready = [S(n) for n in (
        "hist_set", "state_loaded", "pool_stored", "pooled", "poolw_loaded", "y_done", "y_hi", "pooled_ready")]
    sq_ready, sq_summed = S("sq_ready"), S("sq_summed")
    hidden = S("hidden")
    x_again, prompt_gated, sample_gated = S("x_again"), S("prompt_gated"), S("sample_gated")
    x_dve, x_pool, back_zeroed = S("x_dve"), S("x_pool"), S("back_zeroed")
    times_gain, sample_times_gain, shifted, sample_hi, sample_lo = [S(n) for n in (
        "times_gain", "sample_times_gain", "shifted", "sample_hi", "sample_lo")]
    y_stored = S("y_stored")

    def use_of(use, off):
        return off % 4, use + off // 4

    def wait_raw(eng, use, off):
        slot, u = use_of(use, off)
        eng.wait_ge(raw_loaded[slot], 16 * (u + 1))

    def wait_chunk(eng, c4, j):
        eng.wait_ge(half_free, 8 * c4 + (2 * j + 6))

    def quarter_use(g):
        return 2 + 3 * g

    def out_use(n):
        return 2 + 3 * (QUARTERS + Q_GROUPS) + 2 * (U_GROUPS + n)

    def ffn_use(g):
        return out_use(OUT_GROUPS) + 9 * g

    def fill(f):
        if f < 8:
            return Q_C4 + f // 4, 2 + 3 * (QUARTERS + f // 4), DENSE[f % 4], f % 4
        n = f // 4 - 2
        return U_C4 + n, 2 + 3 * (QUARTERS + Q_GROUPS) + 2 * n, SUPER[f % 4], f % 4

    def fill_ada(f):
        c4, use, off, j = fill(f)
        if f < 8:
            nb = 10 + 2 * (f // 4) + j // 2
            return [(nb, off - 2, 2 * (j % 2)), (nb, off - 1, 2 * (j % 2) + 1)], nb if j % 2 else None
        nb = 14 + f // 4 - 2
        return [(nb, off - 1, j)], nb if j == 3 else None

    def seq_view(ap):
        return ap.rearrange("p k (q b) -> p k q b", b=SEQS)

    def bcast_seq(ap9):
        k = ap9.shape[1]
        return ap9[:, :, 1:NSEQ].unsqueeze(2).to_broadcast([P, k, STEPS, SEQS])

    def mod_of(first_block):
        return mod[:, first_block:first_block + 4, :, :].rearrange("p b t s -> p (b t) s")

    GATE1, SCALE2, SHIFT2, GATE2 = 8, 12, 16, 20

    def wait_piece(eng, turn, n):
        who = PIECES[n][0]
        count = sum(1 for p in PIECES[:n + 1] if p[0] == who) + turn * sum(1 for p in PIECES if p[0] == who)
        eng.wait_ge(x_dve if who == "dve" else x_pool, count)

    def update_x(eng, mine, who, done):
        for name, first, end in PIECES:
            if name != who:
                continue
            part = back[:, first:end, :]
            mine.then(eng.tensor_tensor(part, part, rstd[:, :].unsqueeze(1).to_broadcast([P, end - first, T]), ALU.mult))
            eng.tensor_tensor(x[:, first:end, :], x[:, first:end, :], part, ALU.add).then_inc(done, 1)

    block = nc.Block()
    block.__enter__()

    @block.sync
    def _(sp):
        with sp.Fori(0, STREAM // 4) as i:
            for s in range(4):
                sp.wait_ge(slot_used[s], 2 * i + 2)
                sp.dma_start(raw[s][:, :], stream[ds(4 * i + s, 1), :, :].rearrange("a p n -> p (a n)")).then_inc(
                    raw_loaded[s], 16)
        for n, (_, first, end) in enumerate(PIECES):
            wait_piece(sp, 1, n)
            sp.dma_start(y_out[:, first:end, :], x[:, first:end, :]).then_inc(y_stored, 16)
        sp.wait_ge(y_stored, 16 * len(PIECES))

    @block.scalar
    def _(act):
        mine = Steps(act, astep)
        act.dma_start(silu_c[:, :, :], c_cm).then_inc(c_loaded, 16)
        act.dma_start(lam_in[:, :], lam4).then_inc(lam_loaded, 16)
        act.dma_start(x[:, :, :], x_cm).then_inc(x_loaded, 16)
        for dst, src in ((tab[:, :], consts), (gain[:, :], gains), (ada_bias[:, :, :], bias), (cos_sin[:, :, :], trig)):
            act.dma_start(dst, src).then_inc(tables_loaded, 16)

        act.wait_ge(c_loaded, 16)
        act.activation(c_exp[:, :, :], silu_c[:, :, :], ACT.Exp, scale=-1.0).then_inc(c_exped, 1)
        act.wait_ge(lam_summed, 1)
        act.activation(lam_e, bank[6][:, 0:2], ACT.Exp, scale=float(P)).then_inc(lam_exped, 1)

        def square_all(src, loaded, need):
            for g in range(4):
                act.wait_ge(loaded, need(g))
                act.activation(squares[:, 4 * g:4 * g + 4, :], src[:, 4 * g:4 * g + 4, :], ACT.Square).then_inc(squared, 1)

        def root(src, need_mean, width):
            act.wait_ge(meaned, need_mean)
            act.activation(rstd[:, :], src, ACT.Sqrt, bias=eps, scale=1.0 / width).then_inc(rooted, 1)

        def ada_copy(nb, use, off):
            slot, u = use_of(use, off)
            act.wait_ge(slot_used[slot], 2 * u + 4)
            act.wait_ge(sel_done, nb + 1)
            act.activation(ada_rows[:, :], ADA[:, :], ACT.Copy).then_inc(ada_copied, 1)

        def hi_half(c4, use, off, j, h):
            slot, u = use_of(use, off)
            act.wait_ge(raw_loaded[slot], 16 * (u + 1))
            act.wait_ge(half_free, 8 * c4 + (2 * j + h + 1))
            act.activation(w_hi[2 * (j % 2) + h][:, :], raw[slot][:, h * 1024:(h + 1) * 1024], ACT.Copy).then_inc(
                hi_ready, 1)

        def block4(c4, use, offs, following, evac, t, ada_nb=None):
            for j in range(4):
                if j < 3:
                    nxt = (c4, use, offs[j + 1], j + 1)
                else:
                    nxt = following
                if nxt is not None:
                    for h in range(2):
                        hi_half(*nxt, h)
                if j == 3 and ada_nb is not None:
                    ada_copy(ada_nb, use, 6)
                wait_chunk(act, c4, j)
                evac(c4, j, t)

        def freed(ins, j):
            ins.then_inc(bank_free[j % 2], 1)

        square_all(x, x_loaded, lambda g: 16)
        ada_copy(0, 0, 3)
        root(bank[5][:, 0:T], 1, KT)
        ada_copy(1, 1, 3)

        def h_hi_part(count, first):
            act.wait_ge(prompt_mod, count)
            act.wait_ge(sample_mod, count)
            act.activation(h_hi[:, ds(first, 4), :], normed[:, ds(first, 4), :], ACT.Copy).then_inc(h_hi_s, 1)

        h_hi_part(1, 0)
        for h in range(2):
            hi_half(0, quarter_use(0), DENSE[0], 0, h)

        def quarter(g, following, more):
            use = quarter_use(g)
            for j in range(4):
                if j == 3 and more:
                    h_hi_part(g + 2, 4 * g + 4)
                nxt = (g, use, DENSE[j + 1], j + 1) if j < 3 else following
                for h in range(2):
                    hi_half(*nxt, h)
                if j % 2 == 0:
                    ada_copy(2 + 2 * g + j // 2, use, DENSE_ADA[j // 2][3])

        with act.Fori(0, QUARTERS - 1) as g:
            quarter(g, (g + 1, quarter_use(g + 1), DENSE[0], 0), True)
        quarter(QUARTERS - 1, fill(0), False)

        def hi_fill(f, h):
            hi_half(*fill(f), h)

        def ada_fill(f):
            done = fill_ada(f)[1]
            if done is not None:
                ada_copy(done, fill(f)[1], fill(f)[2] - 1)

        def evac_fill(f):
            c4, _, _, j = fill(f)
            wait_chunk(act, c4, j)
            n = f - 8
            if f < 8:
                if f:
                    act.wait_ge(roped, 2 * f)
                freed(act.activation(rope[0][:, :], bank[j % 2][:, 0:T], ACT.Copy), j)
                return
            if n == 0:
                act.wait_ge(hist_set, 1)
            act.activation(u_p[:, n, HIST:UP], bank[n % 2][:, 0:NP_], ACT.Copy)
            freed(act.activation(u_s[:, n, HIST * SEQS:US], bank[n % 2][:, NP_:T], ACT.Copy), n)

        for h in range(2):
            hi_fill(1, h)
        evac_fill(0)
        for t in range(6):
            act.wait_ge(vt_turned, t + 1)
            tile, half = t // 2, t % 2
            if tile < 2:
                dst, src = v_rows[:, tile, half * 512:half * 512 + 512], bank[6 + t % 2][:, :]
            else:
                dst, src = v_new[:, half * 512:half * 512 + 512], bank[6 + t % 2][0:NS, :]
            act.activation(dst, src, ACT.Copy).then_inc(vt_evac, 1)
        for h in range(2):
            hi_fill(2, h)
        ada_fill(1)
        evac_fill(1)

        def exps(h):
            act.wait_ge(negmax, h + 1)
            if h:
                act.wait_ge(t_done, h)
            for m in range(2):
                for qt in range(2):
                    col, width = (0, 128) if qt == 0 else (128, 256)
                    e = act.activation(probs[:, m, col:col + width], bank[5 + m][:, col:col + width], ACT.Exp,
                                       bias=nb4[:, 2 * m + qt:2 * m + qt + 1], scale=SCALE,
                                       accum_out=sums[:, 2 * m + qt:2 * m + qt + 1])
            e.then_inc(exped, 1)

        exps(0)
        for h in range(HEADS):
            f = h + 2
            ada_fill(f)
            act.wait_ge(t_done, h + 1)
            if h:
                act.wait_ge(pv_done, h)
            act.activation(probs_t[:, :], bank[7][:, 0:384], ACT.Copy).then_inc(at_ready, 1)
            if h + 1 < HEADS:
                exps(h + 1)
            hi_fill(f + 1, 0)
            evac_fill(f)
            hi_fill(f + 1, 1)
            act.wait_ge(pv_done, h + 1)
            act.activation(q_cm[:, h, 0:NP_], bank[3][:, 0:NP_], ACT.Copy).then_inc(o_done, 1)
        act.wait_ge(k_stored, 16)
        act.wait_ge(o_done, HEADS)
        act.activation(sub_sq[:, :, 0:NP_], q_cm[:, :, 0:NP_], ACT.Square).then_inc(sub_squared, 1)

        for pr in range(4):
            fills = PAIR_FILLS[pr]
            hi_fill(fills[0] + 1, 0)
            act.wait_ge(dnegmax, pr + 1)
            if pr:
                act.wait_ge(dt_done, pr)
            else:
                act.wait_ge(pv_done, HEADS)
            for t in range(2):
                e = act.activation(dprobs[:, t, :], bank[5 + t][:, 0:T], ACT.Exp, bias=nb4[:, t:t + 1], scale=SCALE,
                                   accum_out=sums[:, t:t + 1])
            e.then_inc(dexped, 1)
            hi_fill(fills[0] + 1, 1)
            ada_fill(fills[0])
            if pr == 1:
                act.wait_ge(sub_copied, 4)
                act.activation(sub_sq[:, :, 0:NP_], sub_sq[:, :, 0:NP_], ACT.Sqrt, bias=eps).then_inc(sub_root, 1)
            evac_fill(fills[0])
            for f in fills[1:]:
                for h in range(2):
                    hi_fill(f + 1, h)
                ada_fill(f)
                evac_fill(f)
            act.wait_ge(dpv_done, pr + 1)
            if pr:
                act.wait_ge(d_turned, pr)
            act.activation(d_rows[:, :], bank[7][:, :], ACT.Copy).then_inc(d_evac, 1)
            act.wait_ge(d_turned, pr + 1)
            for par in range(2):
                got = bank[7][:, :].rearrange("p (t a j r) -> p t a j r", t=2, a=2, j=4)[:, :, par, :, 8 * par:8 * par + 8]
                b = 2 * pr + par
                out = q_cm[:, :, NP_:T].rearrange("p (t j) (q b) -> p t j q b", t=2, b=SEQS)[:, :, :, :, b]
                act.activation(out, got, ACT.Copy).then_inc(d_out, 1)

        act.wait_ge(d_out, 8)
        act.activation(sub_sq[:, :, NP_:T], q_cm[:, :, NP_:T], ACT.Square).then_inc(sub_squared, 1)

        def attn_hi(part, tokens, need):
            act.wait_ge(sub_scaled, need)
            act.activation(m_hi[:, part, tokens], q_cm[:, part, tokens], ACT.Copy).then_inc(sub_hi, 1)

        def pool_hi(n):
            act.wait_ge(y_done, n + 1)
            act.activation(m_hi[:, HEADS + n, :], bank[5 + n % 2][:, 0:T], ACT.Copy,
                           scale=gain[:, G_POOL + n:G_POOL + n + 1]).then_inc(y_hi, 1)

        attn_hi(slice(0, 4), slice(0, NP_), 4)
        attn_hi(slice(4, 8), slice(0, NP_), 4)
        pool_hi(0)
        pool_hi(1)
        act.wait_ge(sub_mean, 5)
        act.activation(sub_sq[:, :, NP_:T], bank[3][:, :].rearrange("p (h t) -> p h t", t=NS), ACT.Sqrt, bias=eps).then_inc(
            sub_root, 1)
        pool_hi(2)
        pool_hi(3)
        attn_hi(slice(0, 8), slice(NP_, T), 5)
        for n in range(4, 8):
            pool_hi(n)

        def evac_out(c4, j, t):
            n = 4 * t + j
            act.activation(back[:, ds(n, 1), :].rearrange("p a t -> p (a t)"), bank[j % 2][:, 0:T], ACT.Copy)
            act.wait_ge(sq_summed, 4 * t + (j + 1))
            freed(act.activation(out_sq[j % 2][:, :], bank[j % 2][:, 0:T], ACT.Square), j)

        def ffn_first(g):
            return (FFN_C4 + 8 * g, ffn_use(g), SUPER[0], 0)

        with act.Fori(0, OUT_GROUPS - 1) as t:
            block4(OUT_C4 + t, out_use(t), SUPER, (OUT_C4 + 1 + t, out_use(t + 1), SUPER[0], 0), evac_out, t, SHIFT2 + t)
        t = OUT_GROUPS - 1
        block4(OUT_C4 + t, out_use(t), SUPER, ffn_first(0), evac_out, t, SHIFT2 + t)

        root(bank[5][:, 0:T], 2, KT)

        def x_times_gain(tiles):
            act.wait_ge(gate_done, 6)
            for k in tiles:
                i = act.activation(normed[:, k, 0:NP_], x[:, k, 0:NP_], ACT.Copy, scale=gate[:, k, 0:1])
            i.then_inc(times_gain, 1)

        for n, (_, first, end) in enumerate(PIECES):
            wait_piece(act, 0, n)
            act.activation(squares[:, first:end, :], x[:, first:end, :], ACT.Square).then_inc(squared, 1)
            if n == 3:
                x_times_gain(range(11, 14))
        x_times_gain(range(14, KT))
        root(bank[5][:, 0:T], 3, KT)
        shift = mod_of(SHIFT2)
        for g in range(4):
            act.wait_ge(normed_s, 4 + g + 1)
            for k in range(4 * g, 4 * g + 4):
                i = act.activation(h_hi[:, k, 0:NP_], normed[:, k, 0:NP_], ACT.Identity, bias=shift[:, k, 0:1])
            i.then_inc(h_hi_s, 1)
            act.wait_ge(sample_mod, 4 + g + 1)
            act.activation(h_hi[:, 4 * g:4 * g + 4, NP_:T], normed[:, 4 * g:4 * g + 4, NP_:T], ACT.Copy).then_inc(sample_hi, 1)

        def evac_ff1(g, c4, j, t):
            act.wait_ge(hidden, 16 * g + 4 * t + (j + 1))
            freed(act.activation(relu[j % 2][:, :], bank[j % 2][:, 0:T], ACT.Relu), j)

        def hi_only(c4, use, following, t, last):
            for j in range(4):
                nxt = (c4, use, PLAIN[j + 1], j + 1) if j < 3 else following
                if nxt is not None:
                    for h in range(2):
                        hi_half(*nxt, h)
                if last:
                    act.wait_ge(bank_free[j % 2], 2 * c4 + (BANK_LEAD + j // 2 + 2))
                    act.wait_ge(sq_summed, 4 * t + (j + KT + 1))
                    act.activation(out_sq[j % 2][:, :], back[:, ds(4 * t + j, 1), :].rearrange("p a t -> p (a t)"),
                                   ACT.Square).then_inc(squared, 1)

        def mlp_group(g, last):
            c4, use = FFN_C4 + 8 * g, ffn_use(g)
            block4(c4, use, SUPER, (c4 + 1, use + 2, 0, 0), lambda c, j, t: evac_ff1(g, c, j, t), 0,
                   GATE2 + g)
            with act.Fori(0, 3) as t:
                block4(c4 + 1 + t, use + 2 + t, PLAIN, (c4 + 2 + t, use + 3 + t, 0, 0),
                       lambda c, j, n: evac_ff1(g, c, j, n), t + 1)
            with act.Fori(0, 3) as t:
                hi_only(c4 + 4 + t, use + 5 + t, (c4 + 5 + t, use + 6 + t, 0, 0), t, last)
            hi_only(c4 + 7, use + 8, None if last else ffn_first(g + 1), 3, last)

        with act.Fori(0, GROUPS - 1) as g:
            mlp_group(g, False)
        mlp_group(GROUPS - 1, True)

        root(bank[5][:, 0:T], 4, KT)

    @block.vector
    def _(dve):
        mine = Steps(dve, dstep)
        dve.memset(ADA[:, :], 0.0).then_inc(slot_used[0], 2)
        dve.memset(ones[:, :], 1.0 / P).then_inc(ones_set, 1)
        mine.mark(dve.memset(eps, EPS))
        mine.mark(dve.memset(coef4, 1.0))
        for n, (sem, by) in enumerate([(slot_used[1], 2), (slot_used[2], 2), (slot_used[3], 2), (half_free, 4), (bank_free[0], 1),
                                       (bank_free[1], 1), (bank_free[2], 1), (bank_free[3], 1), (ada_copied, 1),
                                       (sel_done, 1), (mod_done, 1), (sq_summed, 2), (hidden, 2)]):
            dve.memset(small[:, 32 + n:33 + n], float(n)).then_inc(sem, by)
        dve.wait_ge(c_exped, 1)
        mine.then(dve.tensor_scalar(c_exp[:, :, :], c_exp[:, :, :], 1.0, None, ALU.add))
        mine.then(dve.reciprocal(c_exp[:, :, :], c_exp[:, :, :]))
        dve.tensor_tensor(silu_c[:, :, :], silu_c[:, :, :], c_exp[:, :, :], ALU.mult).then_inc(silu_done, 1)
        dve.wait_ge(lam_loaded, 16)
        dve.tensor_tensor(lam_pr[:, :], lam_in[:, 0:2], lam_in[:, 2:4], ALU.mult).then_inc(lam_pred, 1)
        dve.wait_ge(tables_loaded, 64)
        dve.wait_ge(lam_exped, 1)
        mine.then(dve.tensor_tensor(small[:, 26:27], lam_e[:, 0:1], lam_e[:, 1:2], ALU.subtract))
        mine.then(dve.tensor_scalar(small[:, 27:28], small[:, 26:27], LAM_INIT, -1.0, ALU.add, ALU.mult))
        mine.mark(dve.tensor_scalar(coef4[:, 2:4], coef4[:, 2:4], small[:, 27:28], None, ALU.mult))
        mine.then(dve.scalar_tensor_tensor(coefd, tab[:, C_M1:C_M1 + 1], small[:, 27:28], tab[:, C_M0:C_M0 + 1],
                                           ALU.mult, ALU.add))
        mine.mark(dve.tensor_scalar(gain[:, G_SUB:G_SUB + 1], gain[:, G_SUB:G_SUB + 1], 1.0 - LAM_INIT, None, ALU.mult))

        def invert_root(turn):
            dve.wait_ge(rooted, turn + 1)
            dve.reciprocal(rstd[:, :], rstd[:, :]).then_inc(rstd_s, 1)
            dve.wait_ge(rstd_s, turn + 1)

        def times_rstd(dst, src, g):
            return dve.tensor_tensor(dst[:, 4 * g:4 * g + 4, :], src[:, 4 * g:4 * g + 4, :],
                                     rstd[:, :].unsqueeze(1).to_broadcast([P, 4, T]), ALU.mult)

        def mod_add(nb):
            dve.wait_ge(sel_done, nb + 2)
            dve.tensor_tensor(mod[:, ds(nb, 1), :, :].rearrange("p a t s -> p (a t) s"),
                              MODT[:, 0:64].rearrange("p (t s) -> p t s", s=16)[:, :, 0:NSEQ],
                              ada_bias[:, ds(nb, 1), :].rearrange("p a t -> p (a t)").unsqueeze(2).to_broadcast(
                                  [P, 4, NSEQ]), ALU.add).then_inc(mod_done, 1)

        def lo_half(c4, use, off, j, h):
            slot, u = use_of(use, off)
            dve.wait_ge(hi_ready, 8 * c4 + (2 * j + h + 1))
            q = 2 * (j % 2) + h
            dve.tensor_tensor(w_lo[q][:, :], raw[slot][:, h * 1024:(h + 1) * 1024], w_hi[q][:, :],
                              ALU.subtract).then_inc(slot_used[slot], 1)

        def block4(c4, use, offs, following, evac, t, ada_nb=None):
            for j in range(4):
                nxt = (c4, use, offs[j + 1], j + 1) if j < 3 else following
                if nxt is not None:
                    for h in range(2):
                        lo_half(*nxt, h)
                evac(c4, j, t)
            if ada_nb is not None:
                mod_add(ada_nb)

        def wait_evac(c4, j):
            dve.wait_ge(bank_free[j % 2], 2 * c4 + (BANK_LEAD + j // 2 + 2))

        def scale_gain(first_block, g0):
            dve.scalar_tensor_tensor(gate[:, :, :], mod_of(first_block), 1.0,
                                     gain[:, g0:g0 + KT].unsqueeze(2).to_broadcast([P, KT, NSEQ]),
                                     ALU.add, ALU.mult).then_inc(gate_done, 1)

        def gate_gain(first_block, g0):
            dve.tensor_tensor(gate[:, :, :], mod_of(first_block), gain[:, g0:g0 + KT].unsqueeze(2).to_broadcast(
                [P, KT, NSEQ]), ALU.mult).then_inc(gate_done, 1)

        def low_of_h(count, first):
            dve.wait_ge(h_hi_s, count)
            dve.tensor_tensor(h_lo[:, ds(first, 4), :], normed[:, ds(first, 4), :], h_hi[:, ds(first, 4), :],
                              ALU.subtract).then_inc(h_ready, 1)

        def modulate_quarter(q):
            tiles = ds(4 * q, 4)
            dve.wait_ge(mod_done, 2 * q + 3)
            dve.scalar_tensor_tensor(gate[:, tiles, :], mod[:, ds(2 * q, 1), :, :].rearrange("p a t s -> p (a t) s"), 1.0,
                                     gain[:, ds(4 * q + G_PRE_MIX, 4)].unsqueeze(2).to_broadcast([P, 4, NSEQ]),
                                     ALU.add, ALU.mult).then_inc(gate_done, 1)
            dve.wait_ge(gate_done, q + 1)
            part = normed[:, tiles, 0:NP_]
            mine.then(dve.tensor_tensor(part, part, gate[:, tiles, 0:1].to_broadcast([P, 4, NP_]), ALU.mult))
            dve.tensor_tensor(part, part, mod[:, ds(2 * q + 1, 1), :, 0:1].rearrange("p a t s -> p (a t) s").to_broadcast(
                [P, 4, NP_]), ALU.add).then_inc(prompt_mod, 1)

        invert_root(0)
        for g in range(4):
            times_rstd(normed, x, g).then_inc(normed_s, 1)
        mod_add(0)
        dve.wait_ge(normed_s, 4)
        mod_add(1)
        modulate_quarter(0)
        low_of_h(1, 0)
        for h in range(2):
            lo_half(0, quarter_use(0), DENSE[0], 0, h)
        dve.wait_ge(sums_zeroed, 2)

        def sum_tiles(g, j, h):
            for i in range(2):
                if i == 0:
                    dve.wait_ge(first_done, 8 * g + (2 * j + h + 1))
                else:
                    dve.wait_ge(half_free, 8 * g + (2 * j + h + 5))
                n, b = 4 * (j % 2) + 2 * h + i, 2 * h + i
                tile = v_cm[:, n, :] if j < 2 else k_cm[:, n, :]
                dve.tensor_tensor(tile, QUARTER_BANKS[b][:, 0:T], tile, ALU.add).then_inc(bank_free[b], 1)

        def quarter(g, following, more):
            use = quarter_use(g)
            for j in range(4):
                nxt = (g, use, DENSE[j + 1], j + 1) if j < 3 else following
                if j == 3:
                    mod_add(3 + 2 * g)
                    if more:
                        modulate_quarter(g + 1)
                    sum_tiles(g, j, 0)
                    if more:
                        low_of_h(g + 2, 4 * g + 4)
                lo_half(*nxt, 0)
                if j < 3:
                    lo_half(*nxt, 1)
                    sum_tiles(g, j, 0)
                sum_tiles(g, j, 1)
                if j == 3:
                    lo_half(*nxt, 1)
                if j == 1:
                    mod_add(2 + 2 * g)

        with dve.Fori(0, QUARTERS - 1) as g:
            mine.enter(g, 1)
            quarter(g, (g + 1, quarter_use(g + 1), DENSE[0], 0), True)
        mine.leave(QUARTERS - 1)
        quarter(QUARTERS - 1, fill(0), False)

        swap = list(range(8, 16)) + list(range(8)) + list(range(16, 32))

        def rotate(src, dst, turn):
            if turn:
                dve.wait_ge(roped, turn)
            mine.mark(dve.tensor_tensor(rope[2][:, :], src, cos_sin[:, 0, :], ALU.mult))
            mine.mark(dve.stream_shuffle(rope[1][:, :], src, swap))
            mine.wait()
            mine.then(dve.tensor_tensor(rope[3][:, :], rope[1][:, :], cos_sin[:, 1, :], ALU.mult))
            dve.tensor_tensor(dst, rope[2][:, :], rope[3][:, :], ALU.add).then_inc(roped, 1)

        def rotate_k(f):
            if f == 0:
                for b in range(4):
                    dve.wait_ge(bank_free[b], 4 * QUARTERS + 1)
            if f < 8:
                rotate(k_cm[:, f, :], k_cm[:, f, :], 2 * f)

        def rotate_q(f):
            if f < 8:
                wait_evac(fill(f)[0], fill(f)[3])
                rotate(rope[0][:, :], q_cm[:, f, :], 2 * f + 1)

        def lo_fill(f, h):
            lo_half(*fill(f), h)

        def mod_fill(f):
            if fill_ada(f)[1] is not None:
                mod_add(fill_ada(f)[1])

        def maxima(h):
            dve.wait_ge(s_done, h + 1)
            for m in range(2):
                blocks = bank[5 + m][:, 0:512].rearrange("p (s a k) -> p s a k", s=2, a=2)[:, :, 0, :]
                mine.mark(dve.tensor_tensor(blocks, blocks,
                                            tab[:, C_DIAG:C_DIAG + P].unsqueeze(1).to_broadcast([P, 2, P]), ALU.add))
            mine.wait()
            for m in range(2):
                mine.mark(dve.tensor_reduce(nmax[:, 2 * m:2 * m + 1], bank[5 + m][:, 0:128], AX.X, ALU.max, negate=True))
                mine.mark(dve.tensor_reduce(nmax[:, 2 * m + 1:2 * m + 2], bank[5 + m][:, 128:384], AX.X, ALU.max, negate=True))
            mine.wait()
            dve.tensor_scalar(nb4, nmax, SCALE, None, ALU.mult).then_inc(negmax, 1)

        for f in range(2):
            for h in range(2):
                lo_fill(f + 1, h)
            rotate_k(f)
            rotate_q(f)
            mod_fill(f)
        maxima(0)
        for h in range(HEADS):
            f = h + 2
            dve.wait_ge(exped, h + 1)
            mine.then(dve.reciprocal(rsum, sums))
            mine.then(dve.tensor_tensor(rsum, rsum, coef4, ALU.mult))
            for qt in range(2):
                col, width = (0, 128) if qt == 0 else (128, 256)
                mine.mark(dve.tensor_scalar(probs[:, 0, col:col + width], probs[:, 0, col:col + width],
                                            rsum[:, qt:qt + 1], None, ALU.mult))
            mine.wait()
            for qt in range(2):
                col, width = (0, 128) if qt == 0 else (128, 256)
                last = dve.scalar_tensor_tensor(probs[:, 0, col:col + width], probs[:, 1, col:col + width],
                                                rsum[:, 2 + qt:3 + qt], probs[:, 0, col:col + width], ALU.mult, ALU.add)
            last.then_inc(a_ready, 1)
            rotate_k(f)
            if h + 1 < HEADS:
                maxima(h + 1)
            lo_fill(f + 1, 0)
            rotate_q(f)
            lo_fill(f + 1, 1)
            mod_fill(f)

        def copy_mean(n):
            dve.wait_ge(sub_mean, n + 1)
            dve.tensor_copy(sub_sq[:, 2 * n:2 * n + 2, 0:NP_], bank[3][:, :].rearrange("p (h t) -> p h t", t=NP_)).then_inc(
                sub_copied, 1)

        def sub_norm(part, tokens, roots):
            dve.wait_ge(sub_root, roots)
            mine.then(dve.reciprocal(sub_sq[:, part, tokens], sub_sq[:, part, tokens]))
            dve.scalar_tensor_tensor(q_cm[:, part, tokens], q_cm[:, part, tokens], gain[:, G_SUB:G_SUB + 1],
                                     sub_sq[:, part, tokens], ALU.mult, ALU.mult).then_inc(sub_scaled, 1)

        for pr in range(4):
            fills = PAIR_FILLS[pr]
            dve.wait_ge(ds_done, pr + 1)
            for t in range(2):
                mine.mark(dve.tensor_tensor(bank[5 + t][:, PAST:T], bank[5 + t][:, PAST:T],
                                            tab[:, C_NEWMASK + pr * NS:C_NEWMASK + (pr + 1) * NS], ALU.add))
            mine.wait()
            for t in range(2):
                mine.mark(dve.tensor_reduce(nmax[:, t:t + 1], bank[5 + t][:, 0:T], AX.X, ALU.max, negate=True))
            mine.wait()
            dve.tensor_scalar(nb4[:, 0:2], nmax[:, 0:2], SCALE, None, ALU.mult).then_inc(dnegmax, 1)
            lo_fill(fills[0] + 1, 0)
            dve.wait_ge(dexped, pr + 1)
            mine.then(dve.reciprocal(rsum[:, 0:2], sums[:, 0:2]))
            mine.then(dve.tensor_scalar(rsum[:, 0:2], rsum[:, 0:2], coefd, None, ALU.mult))
            for t in range(2):
                last = dve.tensor_scalar(dprobs[:, t, :], dprobs[:, t, :], rsum[:, t:t + 1], None, ALU.mult)
            last.then_inc(da_ready, 1)
            lo_fill(fills[0] + 1, 1)
            mod_fill(fills[0])
            if pr == 0:
                copy_mean(0)
            dve.wait_ge(dt_done, pr + 1)
            if pr:
                dve.wait_ge(dpv_done, pr)
            for t in range(2):
                dve.tensor_copy(dprobs_t[:, t, :, :].rearrange("p a c -> p (a c)"), bank[5 + t][:, 0:PAST])
                last = dve.tensor_copy(dnew_t[:, t, :], bank[5 + t][0:NS, PAST:PAST + P])
            last.then_inc(dat_ready, 1)
            for f in fills[1:]:
                for h in range(2):
                    lo_fill(f + 1, h)
                mod_fill(f)
            if pr == 0:
                for n in range(1, 4):
                    copy_mean(n)
            if pr:
                for n in ((0, 1), (2,), (3,))[pr - 1]:
                    sub_norm(slice(2 * n, 2 * n + 2), slice(0, NP_), 1)

        def attn_lo(part, tokens, need):
            dve.wait_ge(sub_hi, need)
            dve.tensor_tensor(m_lo[:, part, tokens], q_cm[:, part, tokens], m_hi[:, part, tokens],
                              ALU.subtract).then_inc(attn_ready, 1)

        def pool_lo(n):
            dve.wait_ge(y_hi, n + 1)
            dve.scalar_tensor_tensor(m_lo[:, HEADS + n, :], bank[5 + n % 2][:, 0:T], gain[:, G_POOL + n:G_POOL + n + 1],
                                     m_hi[:, HEADS + n, :], ALU.mult, ALU.subtract).then_inc(pooled_ready, 1)

        attn_lo(slice(0, 4), slice(0, NP_), 1)
        attn_lo(slice(4, 8), slice(0, NP_), 2)
        pool_lo(0)
        pool_lo(1)
        sub_norm(slice(0, 8), slice(NP_, T), 2)
        pool_lo(2)
        pool_lo(3)
        attn_lo(slice(0, 8), slice(NP_, T), 3)
        for n in range(4, 8):
            pool_lo(n)

        dve.wait_ge(mod_done, GATE1 + 5)
        dve.wait_ge(sample_mod, 4)
        gate_gain(GATE1, G_POST_MIX)
        dve.wait_ge(gate_done, 5)
        mine.then(dve.memset(sq_sum[:, :], 0.0))

        def evac_out(c4, j, t):
            wait_evac(c4, j)
            n = 4 * t + j
            dve.tensor_tensor(sq_sum[:, :], sq_sum[:, :], out_sq[j % 2][:, :], ALU.add).then_inc(sq_summed, 1)
            dve.wait_ge(sq_summed, 4 * t + (j + 3))
            if j == 3:
                part = back[:, ds(4 * t, 4), 0:NP_]
                dve.tensor_tensor(part, part, gate[:, ds(4 * t, 4), 0:1].to_broadcast([P, 4, NP_]), ALU.mult).then_inc(
                    prompt_gated, 1)

        def ffn_first(g):
            return (FFN_C4 + 8 * g, ffn_use(g), SUPER[0], 0)

        with dve.Fori(0, OUT_GROUPS - 1) as t:
            block4(OUT_C4 + t, out_use(t), SUPER, (OUT_C4 + 1 + t, out_use(t + 1), SUPER[0], 0), evac_out, t, SHIFT2 + t)
        t = OUT_GROUPS - 1
        block4(OUT_C4 + t, out_use(t), SUPER, ffn_first(0), evac_out, t, SHIFT2 + t)

        dve.wait_ge(mod_done, SCALE2 + 5)
        dve.wait_ge(sample_gated, 4)
        dve.wait_ge(prompt_gated, 4)
        scale_gain(SCALE2, G_PRE_FFN)
        dve.wait_ge(x_again, 16)
        invert_root(1)
        update_x(dve, mine, "dve", x_dve)
        dve.wait_ge(gate_done, 6)
        dve.wait_ge(x_dve, 3)
        for k in range(11):
            mine.mark(dve.tensor_scalar(normed[:, k, 0:NP_], x[:, k, 0:NP_], gate[:, k, 0:1], None, ALU.mult))
        mine.wait()
        dve.wait_ge(times_gain, 2)
        dve.wait_ge(sample_times_gain, 4)
        invert_root(2)
        shift = mod_of(SHIFT2)
        for pair in range(2):
            for g in (2 * pair, 2 * pair + 1):
                times_rstd(normed, normed, g).then_inc(normed_s, 1)
            dve.wait_ge(normed_s, 4 + 2 * pair + 2)
            for g in (2 * pair, 2 * pair + 1):
                dve.wait_ge(h_hi_s, 4 + g + 1)
                for k in range(4 * g, 4 * g + 4):
                    last = dve.scalar_tensor_tensor(h_lo[:, k, 0:NP_], normed[:, k, 0:NP_], shift[:, k, 0:1],
                                                    h_hi[:, k, 0:NP_], ALU.add, ALU.subtract)
                last.then_inc(h_ready, 1)

        def evac_ff1(g, c4, j, t):
            n = 4 * t + j
            wait_evac(c4, j)
            mine.then(dve.tensor_tensor(relu2[j % 2][:, :], relu[j % 2][:, :], relu[j % 2][:, :], ALU.mult))
            hi = m_hi[:, ds(n, 1), :].rearrange("p a t -> p (a t)")
            mine.then(dve.tensor_copy(hi, relu2[j % 2][:, :]))
            dve.tensor_tensor(m_lo[:, ds(n, 1), :].rearrange("p a t -> p (a t)"), relu2[j % 2][:, :], hi,
                              ALU.subtract).then_inc(hidden, 1)

        def evac_ff2(c4, j, t):
            n = 4 * t + j
            wait_chunk(dve, c4, j)
            tile = back[:, ds(n, 1), :].rearrange("p a t -> p (a t)")
            dve.tensor_tensor(tile, bank[j % 2][:, 0:T], tile, ALU.add).then_inc(bank_free[j % 2], 1)

        def evac_last(c4, j, t):
            evac_ff2(c4, j, t)
            dve.wait_ge(squared, 4 * t + (4 + len(PIECES) + j + 1))
            dve.tensor_tensor(sq_sum[:, :], sq_sum[:, :], out_sq[j % 2][:, :], ALU.add).then_inc(sq_summed, 1)
            dve.wait_ge(sq_summed, 4 * t + (j + KT + 3))
            tile = ds(4 * t + j, 1)
            dve.tensor_tensor(seq_view(back[:, tile, NP_:T]), seq_view(back[:, tile, NP_:T]), bcast_seq(gate[:, tile, :]),
                              ALU.mult)
            dve.tensor_tensor(back[:, tile, 0:NP_], back[:, tile, 0:NP_], gate[:, tile, 0:1].to_broadcast([P, 1, NP_]),
                              ALU.mult).then_inc(prompt_gated, 1)

        def mlp_group(g, last):
            c4, use = FFN_C4 + 8 * g, ffn_use(g)
            block4(c4, use, SUPER, (c4 + 1, use + 2, 0, 0), lambda c, j, t: evac_ff1(g, c, j, t), 0,
                   GATE2 + g)
            with dve.Fori(0, 3) as t:
                mine.enter(t, 8)
                block4(c4 + 1 + t, use + 2 + t, PLAIN, (c4 + 2 + t, use + 3 + t, 0, 0),
                       lambda c, j, n: evac_ff1(g, c, j, n), t + 1)
            mine.leave(3)
            dve.wait_ge(back_zeroed, 1)
            evac = evac_ff2
            if last:
                evac = evac_last
                dve.wait_ge(mod_done, GATE2 + 5)
                gate_gain(GATE2, G_POST_FFN)
                dve.wait_ge(gate_done, 7)
                mine.then(dve.memset(sq_sum[:, :], 0.0))
            with dve.Fori(0, 3) as t:
                block4(c4 + 4 + t, use + 5 + t, PLAIN, (c4 + 5 + t, use + 6 + t, 0, 0), evac, t)
            block4(c4 + 7, use + 8, PLAIN, None if last else ffn_first(g + 1), evac, 3)

        outer = Steps(dve, dstep)
        outer.base, outer.n = mine.base, mine.n
        with dve.Fori(0, GROUPS - 1) as g:
            outer.enter(g, 32)
            mine.base, mine.n = outer.base, 0
            mlp_group(g, False)
        mine.base, mine.n = outer.start + (GROUPS - 1) * 32, 0
        mlp_group(GROUPS - 1, True)

        dve.wait_ge(prompt_gated, 4 + KT)
        invert_root(3)
        update_x(dve, mine, "dve", x_dve)

    @block.gpsimd
    def _(pool):
        mine = Steps(pool, pstep)
        pool.dma_start(pages_sb[:, :], table_pg).then_inc(pg_loaded, 16)

        mine.then(pool.memset(k_cm, 0.0))
        pool.memset(small[:, 29:30], 0.0).then_inc(sums_zeroed, 1)
        pool.wait_ge(meaned, 1)
        pool.memset(v_cm[:, :, :], 0.0).then_inc(sums_zeroed, 1)

        def modulate_part(count, gates, g, shift):
            pool.wait_ge(gate_done, gates)
            pool.wait_ge(normed_s, count)
            tiles = slice(4 * g, 4 * g + 4)
            part = seq_view(normed[:, tiles, NP_:T])
            mine.then(pool.tensor_tensor(part, part, bcast_seq(gate[:, tiles, :]), ALU.mult))
            pool.tensor_tensor(part, part, bcast_seq(shift), ALU.add).then_inc(sample_mod, 1)

        modulate_part(1, 1, 0, mod[:, 1, :, :])
        pool.wait_ge(normed_s, 4)
        mine.then(pool.memset(u_p[:, :, 0:HIST], 0.0))
        pool.dma_start(u_s[:, :, 0:HIST * SEQS], state_cm).then_inc(state_loaded, 16)
        pool.wait_ge(state_loaded, 16)
        pool.memset(small[:, 30:31], 0.0).then_inc(hist_set, 1)
        for g in range(1, 4):
            modulate_part(g + 1, g + 1, g, mod[:, 2 * g + 1, :, :])

        for b in range(4):
            pool.wait_ge(bank_free[b], 4 * QUARTERS + 1)
        pool.dma_start(v_out, v_cm[:, :, :]).then_inc(v_stored, 16)
        pool.wait_ge(pg_loaded, 16)
        pool.wait_ge(v_stored, 16)
        pool.wait_ge(vt_evac, 6)

        def load_pages(cache, dst, b, sems):
            for pg in range(PAGES):
                n = b * PAGES + pg
                page = pool.value_load(pages_sb[0:1, n:n + 1], min_val=0, max_val=cache.shape[0] - 1)
                pool.dma_start(dst[:, b % 2, pg, :], cache[ds(page, 1), :, :].rearrange("a p n -> p (a n)")).then_inc(
                    sems[b % 2], 16)

        pool.wait_ge(roped, 10)
        for b in range(2):
            load_pages(kc, k_pages, b, k_loaded)
            load_pages(vc, v_pages, b, v_loaded)
        pool.wait_ge(roped, 16)
        pool.dma_start(k_out, k_cm[:, :, :]).then_inc(k_stored, 16)

        def pool_tile(n):
            pool.wait_ge(bank_free[n % 2], BANK_LEAD + 2 * U_C4 + (n // 2 + 2))
            pool.dma_start(poolp_out[:, n, :], u_p[:, n, NP_:UP]).then_inc(pool_stored, 16)
            pool.dma_start(pools_out[:, n, :], u_s[:, n, STEPS * SEQS:US]).then_inc(pool_stored, 16)
            group = n // 2
            src_p, src_s = u_p[:, n, :], u_s[:, n, :]
            for level in range(group + 1):
                back_by, start = 1 << level, (2 << level) - 1
                dst = win[level % 2]
                mine.mark(pool.tensor_tensor(dst[:, start:UP], src_p[:, start:UP], src_p[:, start - back_by:UP - back_by],
                                             ALU.add))
                mine.then(pool.tensor_tensor(dst[:, UP + start * SEQS:UP + US], src_s[:, start * SEQS:US],
                                             src_s[:, (start - back_by) * SEQS:US - back_by * SEQS], ALU.add))
                src_p, src_s = dst[:, 0:UP], dst[:, UP:UP + US]
            mine.then(pool.tensor_tensor(src_p[:, HIST:HIST + 16], src_p[:, HIST:HIST + 16],
                                         tab[:, C_FIX + 16 * group:C_FIX + 16 * group + 16], ALU.mult))
            mine.mark(pool.tensor_scalar(src_p[:, HIST:UP], src_p[:, HIST:UP], 1.0 / (2 << group), 1.0, ALU.mult, ALU.mult))
            mine.then(pool.tensor_scalar(src_s[:, HIST * SEQS:US], src_s[:, HIST * SEQS:US], 1.0 / (2 << group), 1.0,
                                         ALU.mult, ALU.mult))
            pool.wait_ge(pool_stored, 32 * (n + 1))
            pool.tensor_tensor(u_p[:, n, HIST:UP], src_p[:, HIST:UP], u_p[:, n, HIST:UP], ALU.subtract)
            pool.tensor_tensor(u_s[:, n, HIST * SEQS:US], src_s[:, HIST * SEQS:US], u_s[:, n, HIST * SEQS:US],
                               ALU.subtract).then_inc(pooled, 1)
            pool.wait_ge(pooled, n + 1)

        mine.then(pool.memset(q_pick[:, :, :, :], 0.0))

        def pick_queries(pr):
            for par in range(2):
                b = 2 * pr + par
                for m in range(2):
                    rows = slice(m * HD, (m + 1) * HD)
                    pool.tensor_copy(q_pick[rows, par, :, 16 * par + 8 * m:16 * par + 8 * m + 8],
                                     q_cm[rows, :, NP_ + b:T:SEQS]).then_inc(q_ready, 1)
                    pool.wait_ge(q_ready, 4 * pr + 2 * par + m + 1)

        pick_queries(0)
        pool_tile(0)
        for pr in range(4):
            pool.wait_ge(ds_done, pr + 1)
            if pr < 3:
                for b in (2 * pr + 2, 2 * pr + 3):
                    load_pages(kc, k_pages, b, k_loaded)
                pick_queries(pr + 1)
            for n in ((1, 2), (3, 4), (5,), (6,))[pr]:
                pool_tile(n)
            if pr < 3:
                pool.wait_ge(dpv_done, pr + 1)
                for b in (2 * pr + 2, 2 * pr + 3):
                    load_pages(vc, v_pages, b, v_loaded)
        wait_chunk(pool, U_C4 + 1, 3)
        pool.dma_start(pool_w[:, :, :, :], w_pool).then_inc(poolw_loaded, 16)
        pool_tile(7)
        pool.wait_ge(y_done, 8)
        pool.wait_ge(dpv_done, 4)
        pool.dma_start(x[:, :, :], x_cm).then_inc(x_again, 16)

        pool.wait_ge(gate_done, 5)
        for g in range(4):
            pool.wait_ge(bank_free[1], BANK_LEAD + 2 * (OUT_C4 + g) + 3)
            tiles = slice(4 * g, 4 * g + 4)
            part = seq_view(back[:, tiles, NP_:T])
            pool.tensor_tensor(part, part, bcast_seq(gate[:, tiles, :]), ALU.mult).then_inc(sample_gated, 1)

        def update_pieces(turn, gated):
            pool.wait_ge(prompt_gated, gated)
            pool.wait_ge(rstd_s, 2 * turn + 2)
            update_x(pool, mine, "pool", x_pool)

        pool.wait_ge(sample_gated, 4)
        pool.wait_ge(x_again, 16)
        update_pieces(0, 4)
        pool.wait_ge(gate_done, 6)
        pool.wait_ge(x_dve, 3)
        pool.wait_ge(x_pool, 2)
        for g in range(4):
            tiles = slice(4 * g, 4 * g + 4)
            pool.tensor_tensor(seq_view(normed[:, tiles, NP_:T]), seq_view(x[:, tiles, NP_:T]), bcast_seq(gate[:, tiles, :]),
                               ALU.mult).then_inc(sample_times_gain, 1)
        for pair in range(2):
            for g in (2 * pair, 2 * pair + 1):
                pool.wait_ge(normed_s, 4 + g + 1)
                part = seq_view(normed[:, 4 * g:4 * g + 4, NP_:T])
                pool.tensor_tensor(part, part, bcast_seq(mod[:, SHIFT2 + g, :, :]), ALU.add).then_inc(sample_mod, 1)
            pool.wait_ge(sample_mod, 4 + 2 * pair + 2)
            for g in (2 * pair, 2 * pair + 1):
                tiles = slice(4 * g, 4 * g + 4)
                pool.wait_ge(sample_hi, g + 1)
                pool.tensor_tensor(h_lo[:, tiles, NP_:T], normed[:, tiles, NP_:T], h_hi[:, tiles, NP_:T],
                                   ALU.subtract).then_inc(sample_lo, 1)
        pool.memset(back[:, :, :], 0.0).then_inc(back_zeroed, 1)
        update_pieces(1, 4 + KT)

    @block.tensor
    def _(pe):
        def mean_squares(turn, one=None):
            if one is not None:
                pe.matmul(bank[5][:, 0:T], ones[:, :], one, start=True, stop=True).then_inc(meaned, 1)
                return
            pieces = [(4 * g, 4 * g + 4) for g in range(4)] if turn == 0 else [(a, b) for _, a, b in PIECES]
            for n, (first, end) in enumerate(pieces):
                pe.wait_ge(squared, 4 * turn + n + 1)
                for k in range(first, end):
                    last = pe.matmul(bank[5][:, 0:T], ones[:, :], squares[:, k, :], start=(n == 0 and k == first),
                                     stop=(n == len(pieces) - 1 and k == end - 1))
            last.then_inc(meaned, 1)

        def ada_chunk(nb, use, off, a):
            slot, u = use_of(use, off)
            pe.wait_ge(raw_loaded[slot], 16 * (u + 1))
            if a == 0:
                pe.wait_ge(ada_copied, nb + 1)
            for kk in range(4):
                last = pe.matmul(ADA[32 * kk:32 * kk + NSEQ, :], silu_c[:, 4 * a + kk, :],
                                 raw[slot][:, kk * 512:(kk + 1) * 512], start=(a == 0), stop=(a == 3))
            last.then_inc(slot_used[slot], 2)

        def ada_turn(nb):
            pe.wait_ge(ada_copied, nb + 2)
            pe.wait_ge(mod_done, nb + 1)
            for t in range(4):
                last = pe.matmul(MODT[:, 16 * t:16 * t + NSEQ], ada_rows[:, t * P:(t + 1) * P], tab[:, C_PICK9:C_PICK9 + NSEQ],
                                 start=True, stop=True)
            last.then_inc(sel_done, 1)

        def product_half(c4, use, off, j, h, xh, xl, ready):
            slot, u = use_of(use, off)
            if h == 0:
                pe.wait_ge(bank_free[j % 2], 2 * c4 + (BANK_LEAD + j // 2 + 1))
            ready(h)
            pe.wait_ge(slot_used[slot], 2 * u + (3 + h))
            q = 2 * (j % 2) + h
            for k in range(8):
                for n, (w, v) in enumerate(((w_hi, xh), (w_hi, xl), (w_lo, xh))):
                    last = pe.matmul(bank[j % 2][:, 0:T], w[q][:, k * P:(k + 1) * P], v[:, 8 * h + k, :],
                                     start=(h == 0 and k == 0 and n == 0), stop=(h == 1 and k == 7 and n == 2))
            last.then_inc(half_free, 1)

        def super4(sb_c4, use, nb, xh, xl, ready):
            for j in range(4):
                ada_chunk(nb, use, 2 * j, j)
                for h in range(2):
                    product_half(sb_c4, use, SUPER[j], j, h, xh, xl, ready)
            ada_turn(nb)

        def plain4(c4, use, xh, xl, ready):
            for j in range(4):
                for h in range(2):
                    product_half(c4, use, PLAIN[j], j, h, xh, xl, ready)

        pe.wait_ge(ones_set, 1)
        pe.wait_ge(lam_pred, 1)
        pe.matmul(bank[6][:, 0:2], ones[0:HD, :], lam_pr[:, :], start=True, stop=True).then_inc(lam_summed, 1)
        pe.wait_ge(silu_done, 1)
        for a in range(4):
            ada_chunk(0, 0, a, a)
        mean_squares(0)
        pe.wait_ge(tables_loaded, 64)
        ada_turn(0)
        for a in range(4):
            ada_chunk(1, 1, a, a)
        ada_turn(1)

        def h_wait(turn):
            def wait(h):
                pe.wait_ge(h_ready, 4 * turn + 2 * h + 2)
                if turn:
                    pe.wait_ge(sample_lo, 2 * h + 2)
            return wait

        with pe.Fori(0, QUARTERS) as g:
            use = quarter_use(g)
            for j in range(4):
                for a in (2 * (j % 2), 2 * (j % 2) + 1):
                    ada_chunk(2 + 2 * g + j // 2, use, DENSE_ADA[j // 2][a], a)
                if j == 0:
                    pe.wait_ge(h_ready, g + 1)
                slot, u = use_of(use, DENSE[j])
                for h in range(2):
                    pe.wait_ge(slot_used[slot], 2 * u + (3 + h))
                    q = 2 * (j % 2) + h
                    for i in range(2):
                        pe.wait_ge(bank_free[2 * h + i], 4 * g + (j + 1))
                        for k in range(4):
                            for n, (w, v) in enumerate(((w_hi, h_hi), (w_hi, h_lo), (w_lo, h_hi))):
                                last = pe.matmul(QUARTER_BANKS[2 * h + i][:, 0:T], w[q][:, (4 * i + k) * P:(4 * i + k + 1) * P],
                                                 v[:, ds(4 * g + k, 1), :].rearrange("p a t -> p (a t)"),
                                                 start=(k == 0 and n == 0), stop=(k == 3 and n == 2))
                        last.then_inc(half_free if i else first_done, 1)
                        if j == 3 and h == 0 and i == 0:
                            ada_turn(3 + 2 * g)
                if j == 1:
                    ada_turn(2 + 2 * g)

        def fill_half(f, h):
            c4, use, off, j = fill(f)
            adas, done = fill_ada(f)
            if h == 0:
                for nb, place, a in adas:
                    ada_chunk(nb, use, place, a)
            product_half(c4, use, off, j, h, h_hi, h_lo, h_wait(0))
            if h == 1 and done is not None:
                ada_turn(done)

        for h in range(2):
            fill_half(0, h)
        for b in range(4):
            pe.wait_ge(bank_free[b], 4 * QUARTERS + 1)
        for t in range(6):
            tile, half = t // 2, t % 2
            if t >= 2:
                pe.wait_ge(vt_evac, t - 1)
            rows = P if tile < 2 else NS
            for n in range(4):
                last = pe.transpose(bank[6 + t % 2][0:rows, n * P:(n + 1) * P],
                                    v_cm[:, 4 * half + n, tile * P:tile * P + rows], ident)
            last.then_inc(vt_turned, 1)
        for h in range(2):
            fill_half(1, h)

        def scores(h):
            if h:
                pe.wait_ge(exped, h)
            else:
                pe.wait_ge(vt_evac, 6)
            pe.wait_ge(roped, 2 * h + 2)
            for qt in range(2):
                for m in range(2):
                    rows = slice(m * HD, (m + 1) * HD)
                    col, width = (0, 128) if qt == 0 else (128, 256)
                    last = pe.matmul(bank[5 + m][:, col:col + width], q_cm[rows, h, qt * P:(qt + 1) * P],
                                     k_cm[rows, h, 0:width], start=True, stop=True)
            last.then_inc(s_done, 1)

        scores(0)
        for h in range(HEADS):
            f = h + 2
            fill_half(f, 0)
            pe.wait_ge(a_ready, h + 1)
            if h:
                pe.wait_ge(at_ready, h)
            for n in range(3):
                last = pe.transpose(bank[7][:, n * P:(n + 1) * P], probs[:, 0, n * P:(n + 1) * P], ident)
            last.then_inc(t_done, 1)
            if h + 1 < HEADS:
                scores(h + 1)
            fill_half(f, 1)
            pe.wait_ge(at_ready, h + 1)
            if h:
                pe.wait_ge(o_done, h)
            cols = slice(h * P, (h + 1) * P)
            pe.matmul(bank[3][:, 0:NP_], v_rows[:, 0, cols], probs_t[:, 0:NP_], start=True, stop=False)
            pe.matmul(bank[3][:, P:NP_], v_rows[:, 1, cols], probs_t[:, NP_:384], start=False, stop=True).then_inc(pv_done, 1)

        def sample_scores(pr):
            pe.wait_ge(q_ready, 4 * (pr + 1))
            if pr:
                pe.wait_ge(dat_ready, pr)
            else:
                pe.wait_ge(exped, HEADS)
            for par in range(2):
                pe.wait_ge(k_loaded[par], 32 * (pr + 1))
                for t in range(2):
                    for part in range(2):
                        for j in range(4):
                            h = 4 * t + j
                            if part == 0:
                                out = bank[5 + t][32 * j:32 * j + 32, 0:PAST]
                                rhs = k_pages[:, par, :, h * PAGE:(h + 1) * PAGE]
                            else:
                                out = bank[5 + t][32 * j:32 * j + 32, PAST:T]
                                rhs = k_cm[:, h, NP_:T]
                            last = pe.matmul(out, q_pick[:, par, h, :], rhs, start=(par == 0 and part == 0),
                                             stop=(par == 1 and part == 1), skip_group_check=True)
            last.then_inc(ds_done, 1)

        def mean_of_heads(n):
            pe.wait_ge(sub_squared, 1 if n < 4 else 2)
            if n:
                pe.wait_ge(sub_copied, min(n, 4))
            else:
                pe.wait_ge(o_done, HEADS)
            src = sub_sq[:, 2 * n:2 * n + 2, 0:NP_] if n < 4 else sub_sq[:, :, NP_:T]
            pe.matmul(bank[3][:, :], ones[:, :], src, start=True, stop=True).then_inc(sub_mean, 1)

        sample_scores(0)
        for pr in range(4):
            fills = PAIR_FILLS[pr]
            for h in range(2):
                fill_half(fills[0], h)
            if pr == 0:
                mean_of_heads(0)
            pe.wait_ge(da_ready, pr + 1)
            for t in range(2):
                pick = tab[:, C_PICK:C_PICK + P]
                for pg in range(PAGES):
                    pe.matmul(bank[5 + t][:, pg * PAGE:(pg + 1) * PAGE], dprobs[:, t, pg * PAGE:(pg + 1) * PAGE], pick,
                              start=True, stop=True)
                last = pe.matmul(bank[5 + t][0:NS, PAST:PAST + P], dprobs[:, t, PAST:T], pick, start=True, stop=True)
            last.then_inc(dt_done, 1)
            for f in fills[1:]:
                for h in range(2):
                    fill_half(f, h)
            if pr == 0:
                mean_of_heads(1)
            pe.wait_ge(dat_ready, pr + 1)
            if pr:
                pe.wait_ge(d_out, 2 * pr)
            else:
                pe.wait_ge(at_ready, HEADS)
            for par in range(2):
                pe.wait_ge(v_loaded[par], 32 * (pr + 1))
                for t in range(2):
                    cols = slice((2 * t + par) * P, (2 * t + par + 1) * P)
                    for part in range(PAGES + 1):
                        for j in range(4):
                            h = 4 * t + j
                            if part < PAGES:
                                w, rhs = dprobs_t[:, t, part, 32 * j:32 * j + 32], v_pages[:, par, part, h * P:(h + 1) * P]
                            else:
                                w, rhs = dnew_t[:, t, 32 * j:32 * j + 32], v_new[:, h * P:(h + 1) * P]
                            last = pe.matmul(bank[7][32 * j:32 * j + 32, cols], w, rhs, start=(part == 0),
                                             stop=(part == PAGES), skip_group_check=True)
            last.then_inc(dpv_done, 1)
            if pr == 0:
                mean_of_heads(2)
            if pr < 3:
                sample_scores(pr + 1)
            if pr == 0:
                mean_of_heads(3)
            pe.wait_ge(d_evac, pr + 1)
            for n in range(4):
                last = pe.transpose(bank[7][:, n * P:(n + 1) * P], d_rows[:, n * P:(n + 1) * P], ident)
            last.then_inc(d_turned, 1)

        pe.wait_ge(poolw_loaded, 16)
        for n in range(8):
            g, half = n // 2, n % 2
            if n == 2:
                mean_of_heads(4)
            if n < 2:
                pe.wait_ge(dat_ready, 4)
            else:
                pe.wait_ge(pooled_ready, n - 1)
            pe.wait_ge(pooled, 2 * g + 2)
            out = bank[5 + n % 2]
            for k in range(2):
                w = pool_w[:, g, k, half * P:(half + 1) * P]
                pe.matmul(out[:, 0:NP_], w, u_p[:, 2 * g + k, HIST:UP], start=(k == 0), stop=False, skip_group_check=True)
                last = pe.matmul(out[:, NP_:T], w, u_s[:, 2 * g + k, HIST * SEQS:US], start=False, stop=(k == 1),
                                 skip_group_check=True)
            last.then_inc(y_done, 1)

        def mix_wait(h):
            if h == 0:
                pe.wait_ge(attn_ready, 3)
            else:
                pe.wait_ge(pooled_ready, 8)

        with pe.Fori(0, OUT_GROUPS) as t:
            super4(OUT_C4 + t, out_use(t), SHIFT2 + t, m_hi, m_lo, mix_wait)
        pe.wait_ge(sq_summed, 2 + KT)
        mean_squares(1, sq_sum[:, :])
        mean_squares(1)

        def hidden_wait(g):
            return lambda h: pe.wait_ge(hidden, 16 * g + (2 + 8 * h + 8))

        with pe.Fori(0, GROUPS) as g:
            c4, use = FFN_C4 + 8 * g, ffn_use(g)
            super4(c4, use, GATE2 + g, h_hi, h_lo, h_wait(1))
            with pe.Fori(0, 3) as t:
                plain4(c4 + 1 + t, use + 2 + t, h_hi, h_lo, h_wait(1))
            with pe.Fori(0, 4) as t:
                plain4(c4 + 4 + t, use + 5 + t, m_hi, m_lo, hidden_wait(g))
        pe.wait_ge(sq_summed, 2 + 2 * KT)
        mean_squares(2, sq_sum[:, :])

    block.__exit__(None, None, None)


def shape_tables():
    tab = np.zeros((P, C_END), np.float32)
    rows = np.arange(P)
    tab[:, C_ID:C_ID + P] = np.eye(P)
    tab[:, C_DIAG:C_DIAG + P] = np.where(rows[None, :] <= rows[:, None], 0.0, MASKED)
    par, m, q = rows // 16 % 2, rows // 8 % 2, rows % 8
    key_q, key_b = np.arange(NS) // SEQS, np.arange(NS) % SEQS
    for pr in range(4):
        seen = (key_b[None, :] == 2 * pr + par[:, None]) & (key_q[None, :] <= q[:, None])
        tab[:, C_NEWMASK + pr * NS:C_NEWMASK + (pr + 1) * NS] = np.where(seen, 0.0, MASKED)
    for s in range(NSEQ):
        tab[s::32, C_PICK9 + s] = 1.0
    tab[rows, C_PICK + rows // 32 * 32 + par * 8 + q] = 1.0
    tab[:, C_M0], tab[:, C_M1] = m == 0, m == 1
    for g in range(POOL_GROUPS):
        w = 2 << g
        tab[:, C_FIX + 16 * g:C_FIX + 16 * g + 16] = w / np.minimum(w, np.arange(16) + 1)
    rot = HD // 4
    inv = (np.float32(1.0) / np.float32(500000.0) ** (np.arange(0, rot, 2, dtype=np.float32) / np.float32(rot))).astype(np.float32)
    pos = np.concatenate([np.arange(NP_), PAST + np.repeat(np.arange(STEPS), SEQS)]).astype(np.float32)
    trig = np.zeros((P, 2, T), np.float32)
    trig[:, 0] = 1.0
    for p in range(P):
        d = p % HD
        if d < rot:
            ang = (pos * inv[d % (rot // 2)]).astype(np.float32)
            trig[p, 0] = np.cos(ang)
            trig[p, 1] = np.sin(ang) * (-1.0 if d < rot // 2 else 1.0)
    return tab, trig


ADA_ORDER = [(1 - n % 2, n // 2) for n in range(8)] + [(part, n) for part in (2, 4, 3, 5) for n in range(4)]


def weight_stream(w_ada, w_in, w_out, w_ff1, w_ff2):
    def ada_block(nb):
        part, column = ADA_ORDER[nb]
        first = part * D + column * 512
        part = w_ada[:, first:first + 512].reshape(4, 4, P, 512)
        return [part[a].transpose(1, 0, 2).reshape(P, 2048) for a in range(4)]

    def chunk(w, col, row=0):
        return w[row:row + D, col * P:(col + 1) * P].reshape(KT, P, P).transpose(1, 0, 2).reshape(P, 2048)

    def quarter_chunk(g, tiles):
        rows = w_in[g * 512:(g + 1) * 512]
        return np.concatenate([rows[:, c * P:(c + 1) * P].reshape(4, P, P).transpose(1, 0, 2).reshape(P, 512)
                               for c in tiles], axis=1)

    def place(products, places, blocks):
        ada = [c for nb in blocks for c in ada_block(nb)]
        out = []
        for n in range(len(products) + len(ada)):
            out.append(products[places.index(n)] if n in places else ada.pop(0))
        return out

    first_q, first_k, first_v, first_u = 0, 8, 16, 24
    vk = [first_v + n for n in range(8)] + [first_k + n for n in range(8)]
    chunks = ada_block(0) + ada_block(1)
    for g in range(QUARTERS):
        chunks += place([quarter_chunk(g, vk[4 * j:4 * j + 4]) for j in range(4)], DENSE, (2 + 2 * g, 3 + 2 * g))
    for n in range(Q_GROUPS):
        chunks += place([chunk(w_in, first_q + 4 * n + j) for j in range(4)], DENSE, (10 + 2 * n, 11 + 2 * n))
    for n in range(U_GROUPS):
        chunks += place([chunk(w_in, first_u + 4 * n + j) for j in range(4)], SUPER, (14 + n,))
    for n in range(OUT_GROUPS):
        chunks += place([chunk(w_out, 4 * n + j) for j in range(4)], SUPER, (16 + n,))
    for g in range(GROUPS):
        up = [chunk(w_ff1, 16 * g + n) for n in range(16)]
        chunks += place(up[:4], SUPER, (20 + g,)) + up[4:] + [chunk(w_ff2, n, g * D) for n in range(16)]
    assert len(chunks) == STREAM
    return np.stack(chunks)


def channel_major(rows):
    return np.ascontiguousarray(rows.reshape(rows.shape[0], -1, P).transpose(2, 1, 0))


def kernel(**inputs):
    import concourse.bacc as bacc
    from concourse.bass_utils import run_bass_kernel_spmd

    a = {k: np.asarray(v) for k, v in inputs.items()}
    xs = a["x_sample"].transpose(1, 0, 2).reshape(NS, D)
    tab, trig = shape_tables()
    n_phys = a["cache_k"].shape[1]
    arrays = {
        "stream": weight_stream(a["w_ada"][0], a["w_in"][0], a["w_out"][0], a["w_ff1"][0], a["w_ff2"][0]),
        "x_cm": channel_major(np.concatenate([a["x_prompt"][0], xs])),
        "c_cm": channel_major(np.concatenate([a["c_prompt"], a["c_sample"]])),
        "kc": np.ascontiguousarray(a["cache_k"][0].transpose(0, 3, 2, 1)).reshape(n_phys, P, HEADS * PAGE),
        "vc": a["cache_v"][0].reshape(n_phys, PAGE, HEADS * P),
        "table_pg": a["page_table"].reshape(1, SEQS * PAGES),
        "state_cm": np.ascontiguousarray(a["state_pool"][0].reshape(SEQS, HIST, 8, P).transpose(3, 2, 1, 0)).reshape(
            P, 8, HIST * SEQS),
        "w_pool": np.ascontiguousarray(a["w_pool"][0].reshape(POOL_GROUPS, 2, P, 256).transpose(2, 0, 1, 3)),
        "bias": np.ascontiguousarray(
            a["b_ada"][0].reshape(6, 4, 4, P)[[p for p, _ in ADA_ORDER], [n for _, n in ADA_ORDER]].transpose(2, 0, 1)),
        "gains": np.ascontiguousarray(np.concatenate(
            [a[n][0].reshape(-1, P) for n in ("g_pre_mix", "g_post_mix", "g_pre_ffn", "g_post_ffn", "pool_scale", "g_subln")]).T),
        "lam4": np.ascontiguousarray(np.stack([a[n][0] for n in ("lambda_q1", "lambda_q2", "lambda_k1", "lambda_k2")], 1)),
        "trig": trig,
        "consts": tab,
    }
    outs = {"y_out": (P, KT, T), "k_out": (P, HEADS, T), "v_out": (P, HEADS, T), "poolp_out": (P, 8, HIST),
            "pools_out": (P, 8, HIST * SEQS)}
    nc = bacc.Bacc("TRN2", target_bir_lowering=False, num_devices=1)
    args = [nc.dram_tensor("in_" + n, v.shape, mybir.dt.from_np(v.dtype), kind="ExternalInput").ap() for n, v in arrays.items()]
    args += [nc.dram_tensor(n, s, mybir.dt.float32, kind="ExternalOutput").ap() for n, s in outs.items()]
    decoder_step(nc, *args)
    got = run_bass_kernel_spmd(nc, [{"in_" + n: v for n, v in arrays.items()}], core_ids=[0]).results[0]

    def rows(cm):
        r = cm.transpose(2, 1, 0).reshape(T, -1)
        return r[:NP_], r[NP_:].reshape(STEPS, SEQS, -1).transpose(1, 0, 2)

    y_p, y_s = rows(got["y_out"])
    k_p, k_s = rows(got["k_out"])
    v_p, v_s = rows(got["v_out"])
    pool_p = got["poolp_out"].transpose(2, 1, 0).reshape(1, 1, HIST, 8 * P)
    pool_s = got["pools_out"].reshape(P, 8, HIST, SEQS).transpose(3, 2, 1, 0).reshape(1, SEQS, HIST, 8 * P)
    return (y_p[None], y_s, k_p.reshape(1, 1, NP_, HEADS, P), v_p.reshape(1, 1, NP_, HEADS, P), pool_p,
            k_s.reshape(1, SEQS, STEPS, HEADS, P), v_s.reshape(1, SEQS, STEPS, HEADS, P), pool_s)
```
